# Optimizing a Trainium2 kernel written in Bass

```python
import jax
import jax.numpy as jnp
from jax import lax
import numpy as np

D_MODEL = 1024
BATCH = 1
SEQ = 512
DEPTH = 1
DEC_BATCH = 8
DEC_SEQ = 1
PAST_LEN = 4096
PAGE_SIZE = 128

HEAD_DIM = 64
W_MIX = D_MODEL
W_ATT = W_MIX // 2
W_MLSTM = W_MIX - W_ATT
H_ATT = W_ATT // HEAD_DIM
H_MLSTM = W_MLSTM // HEAD_DIM
DILATIONS = ((128, 1), (512, 4), (2048, 16))
MAX_WINDOW = 2048
ATT_BLOCK = 128
ROPE_THETA = 10000.0
CONV_W = 4
MLSTM_CHUNK = 64
PEER_HEADS = 8
PEER_NKEYS = 128
PEER_EXPERTS = PEER_NKEYS * PEER_NKEYS
PEER_DKEY = 256
PEER_TOPK = 16
PEER_BLOCK = 256
PROJ_SIZES = (W_ATT, W_ATT, W_ATT, 2 * W_MLSTM, W_MLSTM, 2 * H_MLSTM, W_MLSTM)
PROJ = sum(PROJ_SIZES)
EPS = 1e-6
NEG = -1e30

kernel_name = 'hymba_dilated_mlstm_peer_step'

def rms_norm(x, g):
    xf = x.astype(jnp.float32)
    y = xf * lax.rsqrt(jnp.mean(xf * xf, axis=-1, keepdims=True) + EPS)
    return (y * g.astype(jnp.float32)).astype(x.dtype)

def rope(x, pos):
    half = HEAD_DIM // 2
    inv = ROPE_THETA ** (-jnp.arange(half, dtype=jnp.float32) / half)
    ang = pos.astype(jnp.float32)[:, None] * inv[None, :]
    cos = jnp.cos(ang)[None, :, None, :]
    sin = jnp.sin(ang)[None, :, None, :]
    xf = x.astype(jnp.float32)
    x1, x2 = xf[..., :half], xf[..., half:]
    return jnp.concatenate([x1 * cos - x2 * sin, x1 * sin + x2 * cos], axis=-1).astype(x.dtype)

def in_projection(x, norm_g, w_in):
    z = jnp.einsum('btd,dp->btp', rms_norm(x, norm_g), w_in)
    offs = [int(o) for o in np.cumsum((0,) + PROJ_SIZES)]
    return tuple(z[..., offs[i]:offs[i + 1]] for i in range(len(PROJ_SIZES)))

def attn_qkv(aq, ak, av, pos, qn_g, kn_g):
    B, T = aq.shape[:2]
    q = rope(rms_norm(aq.reshape(B, T, H_ATT, HEAD_DIM), qn_g), pos)
    k = rope(rms_norm(ak.reshape(B, T, H_ATT, HEAD_DIM), kn_g), pos)
    v = av.reshape(B, T, H_ATT, HEAD_DIM)
    return q, k, v

def dilated_branch_prompt(q, k, v, window, dilation):
    B, S, H, Dh = q.shape
    span = window // dilation
    L = S // dilation
    nb = -(-L // ATT_BLOCK)
    Lp = nb * ATT_BLOCK

    def to_blocks(t):
        t = t.reshape(B, L, dilation, H, Dh)
        t = jnp.pad(t, ((0, 0), (0, Lp - L), (0, 0), (0, 0), (0, 0)))
        return t.reshape(B, nb, ATT_BLOCK, dilation, H, Dh)

    def with_prev(t):
        prev = jnp.pad(t[:, :-1], ((0, 0), (1, 0), (0, 0), (0, 0), (0, 0), (0, 0)))
        return jnp.concatenate([prev, t], axis=2)

    qb = to_blocks(q)
    kb = with_prev(to_blocks(k))
    vb = with_prev(to_blocks(v))
    s = jnp.einsum('bnqrhd,bnkrhd->bnrhqk', qb, kb).astype(jnp.float32) * (HEAD_DIM ** -0.5)
    blk = jnp.arange(nb)[:, None]
    qi = blk * ATT_BLOCK + jnp.arange(ATT_BLOCK)[None, :]
    ki = (blk - 1) * ATT_BLOCK + jnp.arange(2 * ATT_BLOCK)[None, :]
    dist = qi[:, :, None] - ki[:, None, :]
    mask = (dist >= 0) & (dist <= span) & (ki[:, None, :] >= 0)
    s = jnp.where(mask[None, :, None, None], s, NEG)
    m = jnp.max(s, axis=-1, keepdims=True)
    p = jnp.exp(s - m)
    l = jnp.sum(p, axis=-1, keepdims=True)
    o = jnp.einsum('bnrhqk,bnkrhd->bnqrhd', p / l, vb.astype(jnp.float32))
    o = o.reshape(B, Lp, dilation, H, Dh)[:, :L].reshape(B, S, H, Dh)
    lse = (m + jnp.log(l))[..., 0]
    lse = jnp.transpose(lse, (0, 1, 4, 2, 3)).reshape(B, Lp, dilation, H)[:, :L].reshape(B, S, H)
    return o, lse

def dilated_branch_sample(q, k_all, v_all, base, window, dilation):
    span = window // dilation
    T = q.shape[1]
    qpos = PAST_LEN + jnp.arange(T)
    kpos = qpos[:, None] - dilation * jnp.arange(span + 1)[None, :]
    valid = kpos >= base
    idx = jnp.clip(kpos - base, 0, k_all.shape[1] - 1)
    kg = k_all[:, idx]
    vg = v_all[:, idx]
    s = jnp.einsum('bthd,btjhd->bthj', q, kg).astype(jnp.float32) * (HEAD_DIM ** -0.5)
    s = jnp.where(valid[None, :, None, :], s, NEG)
    m = jnp.max(s, axis=-1, keepdims=True)
    p = jnp.exp(s - m)
    l = jnp.sum(p, axis=-1, keepdims=True)
    o = jnp.einsum('bthj,btjhd->bthd', p / l, vg.astype(jnp.float32))
    return o, (m + jnp.log(l))[..., 0]

def merge_branches(outs, lses):
    w = jax.nn.softmax(jnp.stack(lses, axis=0), axis=0)
    return jnp.einsum('nbth,nbthd->bthd', w, jnp.stack(outs, axis=0))

def mlstm_scan(q, k, v, ig, lf, C0, n0, m0, chunk):
    B, T, H, Dh = q.shape
    nc = T // chunk

    def chunks(t):
        t = t.astype(jnp.float32)
        return jnp.moveaxis(t.reshape((B, nc, chunk) + t.shape[2:]), 1, 0)

    causal = jnp.tril(jnp.ones((chunk, chunk), dtype=bool))

    def step(carry, inp):
        C, n, m = carry
        qc, kc, vc, igc, lfc = inp
        b = jnp.cumsum(lfc, axis=1)
        log_d = b[:, :, None, :] - b[:, None, :, :] + igc[:, None, :, :]
        log_d = jnp.where(causal[None, :, :, None], log_d, NEG)
        m_inter = b + m[:, None, :]
        m_t = jnp.maximum(m_inter, jnp.max(log_d, axis=2))
        sd = jnp.einsum('bthd,bshd->btsh', qc, kc) * jnp.exp(log_d - m_t[:, :, None, :])
        scale_inter = jnp.exp(m_inter - m_t)
        num = scale_inter[..., None] * jnp.einsum('bhvk,bthk->bthv', C, qc) + jnp.einsum('btsh,bshv->bthv', sd, vc)
        den = scale_inter * jnp.einsum('bhk,bthk->bth', n, qc) + jnp.sum(sd, axis=2)
        h = num / jnp.maximum(jnp.abs(den), jnp.exp(-m_t))[..., None]
        m_new = m_t[:, -1]
        decay = jnp.exp(b[:, -1] + m - m_new)
        w_s = jnp.exp(b[:, -1:] - b + igc - m_new[:, None])
        C_new = decay[..., None, None] * C + jnp.einsum('bsh,bshv,bshk->bhvk', w_s, vc, kc)
        n_new = decay[..., None] * n + jnp.einsum('bsh,bshk->bhk', w_s, kc)
        return (C_new, n_new, m_new), h

    carry0 = (C0.astype(jnp.float32), n0.astype(jnp.float32), m0.astype(jnp.float32))
    (C, n, m), hs = lax.scan(step, carry0, (chunks(q), chunks(k), chunks(v), chunks(ig), chunks(lf)))
    h = jnp.moveaxis(hs, 0, 1).reshape(B, T, H, Dh)
    return h, C, n, m

def mlstm_mixer(mqk, mv, mg, mo, conv_buf, C0, n0, m0, conv_w, conv_b, b_gates, norm_g, chunk):
    B, T = mqk.shape[:2]
    xcat = jnp.concatenate([conv_buf.astype(mqk.dtype), mqk], axis=1)
    conv = conv_b + conv_w[0] * xcat[:, 0:T]
    for j in range(1, CONV_W):
        conv = conv + conv_w[j] * xcat[:, j:j + T]
    qk = jax.nn.silu(conv)
    q = qk[..., :W_MLSTM].reshape(B, T, H_MLSTM, HEAD_DIM)
    k = qk[..., W_MLSTM:].reshape(B, T, H_MLSTM, HEAD_DIM) * (HEAD_DIM ** -0.5)
    v = mv.reshape(B, T, H_MLSTM, HEAD_DIM)
    gates = mg.astype(jnp.float32) + b_gates.astype(jnp.float32)
    ig = gates[..., :H_MLSTM]
    lf = jax.nn.log_sigmoid(gates[..., H_MLSTM:])
    h, C, n, m = mlstm_scan(q, k, v, ig, lf, C0, n0, m0, chunk)
    h = rms_norm(h, norm_g.reshape(H_MLSTM, HEAD_DIM)).reshape(B, T, W_MLSTM)
    out = (jax.nn.sigmoid(mo.astype(jnp.float32)) * h).astype(mqk.dtype)
    return out, C, n, m, xcat[:, T:]

def peer_ffn(h, w_query, qnorm_g, subkeys, u, v):
    B, T, D = h.shape
    n = B * T
    nblk = -(-n // PEER_BLOCK)
    hb_all = jnp.pad(h.reshape(n, D), ((0, nblk * PEER_BLOCK - n), (0, 0))).reshape(nblk, PEER_BLOCK, D)
    half = PEER_DKEY // 2

    def block(hb):
        q = rms_norm(jnp.einsum('td,dq->tq', hb, w_query).reshape(PEER_BLOCK, PEER_HEADS, PEER_DKEY), qnorm_g)
        s1 = jnp.einsum('thc,hnc->thn', q[..., :half], subkeys[:, 0]).astype(jnp.float32)
        s2 = jnp.einsum('thc,hnc->thn', q[..., half:], subkeys[:, 1]).astype(jnp.float32)
        v1, i1 = lax.top_k(s1, PEER_TOPK)
        v2, i2 = lax.top_k(s2, PEER_TOPK)
        cand = (v1[..., :, None] + v2[..., None, :]).reshape(PEER_BLOCK, PEER_HEADS, PEER_TOPK * PEER_TOPK)
        sc, ci = lax.top_k(cand, PEER_TOPK)
        e = (jnp.take_along_axis(i1, ci // PEER_TOPK, axis=-1) * PEER_NKEYS
             + jnp.take_along_axis(i2, ci % PEER_TOPK, axis=-1))
        g = jax.nn.softmax(sc, axis=-1).reshape(PEER_BLOCK, PEER_HEADS * PEER_TOPK)
        e = e.reshape(PEER_BLOCK, PEER_HEADS * PEER_TOPK)
        a = jax.nn.gelu(jnp.einsum('td,ted->te', hb, u[e]).astype(jnp.float32), approximate=False)
        return jnp.einsum('te,ted->td', (g * a).astype(hb.dtype), v[e])

    out = lax.map(block, hb_all).reshape(nblk * PEER_BLOCK, D)[:n]
    return out.reshape(B, T, D)

def layer_output(x, att, mh, w_out, norm2_g, w_query, qnorm_g, subkeys, u, v):
    B, T = x.shape[:2]
    mix = jnp.concatenate([att.reshape(B, T, W_ATT).astype(x.dtype), mh], axis=-1)
    x = x + jnp.einsum('btm,md->btd', mix, w_out)
    return x + peer_ffn(rms_norm(x, norm2_g), w_query, qnorm_g, subkeys, u, v)

def setup_inputs(seed: int = 0) -> dict:
    key = jax.random.key(seed)
    ks = jax.random.split(key, 24)
    f32 = jnp.float32

    def nrm(k, shape, scale):
        return scale * jax.random.normal(k, shape, f32)

    wb = min(MAX_WINDOW, PAST_LEN)
    forget_bias = jnp.linspace(3.0, 6.0, H_MLSTM, dtype=f32)
    b_gates = jnp.concatenate([nrm(ks[8], (DEPTH, H_MLSTM), 0.1),
                               forget_bias[None, :] + nrm(ks[9], (DEPTH, H_MLSTM), 0.1)], axis=-1)
    return {
        'x_prompt': nrm(ks[0], (BATCH, SEQ, D_MODEL), 1.0),
        'x_sample': nrm(ks[1], (DEC_BATCH, DEC_SEQ, D_MODEL), 1.0),
        'cache_attn_k': nrm(ks[2], (DEPTH, DEC_BATCH, wb, H_ATT, HEAD_DIM), 1.0),
        'cache_attn_v': nrm(ks[3], (DEPTH, DEC_BATCH, wb, H_ATT, HEAD_DIM), 1.0),
        'state_mlstm_C': nrm(ks[4], (DEPTH, DEC_BATCH, H_MLSTM, HEAD_DIM, HEAD_DIM), 0.1),
        'state_mlstm_n': nrm(ks[5], (DEPTH, DEC_BATCH, H_MLSTM, HEAD_DIM), 0.1),
        'state_mlstm_m': nrm(ks[6], (DEPTH, DEC_BATCH, H_MLSTM), 0.5),
        'state_mlstm_conv': nrm(ks[7], (DEPTH, DEC_BATCH, CONV_W - 1, 2 * W_MLSTM), 1.0),
        'norm1_g': 1.0 + nrm(ks[10], (DEPTH, D_MODEL), 0.02),
        'w_in': nrm(ks[11], (DEPTH, D_MODEL, PROJ), D_MODEL ** -0.5),
        'att_qnorm_g': 1.0 + nrm(ks[12], (DEPTH, HEAD_DIM), 0.02),
        'att_knorm_g': 1.0 + nrm(ks[13], (DEPTH, HEAD_DIM), 0.02),
        'b_gates': b_gates,
        'mlstm_conv_w': nrm(ks[14], (DEPTH, CONV_W, 2 * W_MLSTM), CONV_W ** -0.5),
        'mlstm_conv_b': nrm(ks[15], (DEPTH, 2 * W_MLSTM), 0.02),
        'mlstm_norm_g': 1.0 + nrm(ks[16], (DEPTH, W_MLSTM), 0.02),
        'w_out': nrm(ks[17], (DEPTH, W_MIX, D_MODEL), W_MIX ** -0.5),
        'norm2_g': 1.0 + nrm(ks[18], (DEPTH, D_MODEL), 0.02),
        'peer_w_query': nrm(ks[19], (DEPTH, D_MODEL, PEER_HEADS * PEER_DKEY), D_MODEL ** -0.5),
        'peer_qnorm_g': 1.0 + nrm(ks[20], (DEPTH, PEER_DKEY), 0.02),
        'peer_subkeys': nrm(ks[21], (DEPTH, PEER_HEADS, 2, PEER_NKEYS, PEER_DKEY // 2), (PEER_DKEY // 2) ** -0.5),
        'peer_u': nrm(ks[22], (DEPTH, PEER_EXPERTS, D_MODEL), D_MODEL ** -0.5),
        'peer_v': nrm(ks[23], (DEPTH, PEER_EXPERTS, D_MODEL), PEER_HEADS ** -0.5),
    }

def reference(x_prompt, x_sample, cache_attn_k, cache_attn_v, state_mlstm_C, state_mlstm_n, state_mlstm_m,
              state_mlstm_conv, norm1_g, w_in, att_qnorm_g, att_knorm_g, b_gates, mlstm_conv_w, mlstm_conv_b,
              mlstm_norm_g, w_out, norm2_g, peer_w_query, peer_qnorm_g, peer_subkeys, peer_u, peer_v):
    B, S = x_prompt.shape[:2]
    DB, DS = x_sample.shape[:2]
    wb_prompt = min(MAX_WINDOW, S)
    base = PAST_LEN - cache_attn_k.shape[2]
    pos_p = jnp.arange(S, dtype=jnp.int32)
    pos_s = PAST_LEN + jnp.arange(DS, dtype=jnp.int32)
    chunk_p = min(MLSTM_CHUNK, S)
    dt = x_prompt.dtype
    xp, xs = x_prompt, x_sample
    kp_l, vp_l, ks_l, vs_l = [], [], [], []
    cp_l, n_p_l, mp_l, bp_l = [], [], [], []
    cs_l, n_s_l, ms_l, bs_l = [], [], [], []
    for li in range(DEPTH):
        pw = (peer_w_query[li], peer_qnorm_g[li], peer_subkeys[li], peer_u[li], peer_v[li])
        mw = (mlstm_conv_w[li], mlstm_conv_b[li], b_gates[li], mlstm_norm_g[li])

        aq, ak, av, mqk, mv, mg, mo = in_projection(xp, norm1_g[li], w_in[li])
        q, k, v = attn_qkv(aq, ak, av, pos_p, att_qnorm_g[li], att_knorm_g[li])
        res = [dilated_branch_prompt(q, k, v, w, d) for (w, d) in DILATIONS]
        att = merge_branches([r[0] for r in res], [r[1] for r in res])
        zC = jnp.zeros((B, H_MLSTM, HEAD_DIM, HEAD_DIM), dt)
        zn = jnp.zeros((B, H_MLSTM, HEAD_DIM), dt)
        zm = jnp.zeros((B, H_MLSTM), dt)
        zconv = jnp.zeros((B, CONV_W - 1, 2 * W_MLSTM), dt)
        mh, C, n, m, cb = mlstm_mixer(mqk, mv, mg, mo, zconv, zC, zn, zm, *mw, chunk_p)
        xp = layer_output(xp, att, mh, w_out[li], norm2_g[li], *pw)
        kp_l.append(k[:, S - wb_prompt:])
        vp_l.append(v[:, S - wb_prompt:])
        cp_l.append(C.astype(dt))
        n_p_l.append(n.astype(dt))
        mp_l.append(m.astype(dt))
        bp_l.append(cb)

        aq, ak, av, mqk, mv, mg, mo = in_projection(xs, norm1_g[li], w_in[li])
        q, k, v = attn_qkv(aq, ak, av, pos_s, att_qnorm_g[li], att_knorm_g[li])
        k_all = jnp.concatenate([cache_attn_k[li].astype(k.dtype), k], axis=1)
        v_all = jnp.concatenate([cache_attn_v[li].astype(v.dtype), v], axis=1)
        res = [dilated_branch_sample(q, k_all, v_all, base, w, d) for (w, d) in DILATIONS]
        att = merge_branches([r[0] for r in res], [r[1] for r in res])
        mh, C, n, m, cb = mlstm_mixer(mqk, mv, mg, mo, state_mlstm_conv[li], state_mlstm_C[li],
                                      state_mlstm_n[li], state_mlstm_m[li], *mw, DS)
        xs = layer_output(xs, att, mh, w_out[li], norm2_g[li], *pw)
        ks_l.append(k)
        vs_l.append(v)
        cs_l.append(C.astype(dt))
        n_s_l.append(n.astype(dt))
        ms_l.append(m.astype(dt))
        bs_l.append(cb)

    new_k_prompt = jnp.stack(kp_l)
    new_v_prompt = jnp.stack(vp_l)
    new_k_sample = jnp.stack(ks_l)
    new_v_sample = jnp.stack(vs_l)
    new_C_prompt = jnp.stack(cp_l)
    new_n_prompt = jnp.stack(n_p_l)
    new_m_prompt = jnp.stack(mp_l)
    new_conv_prompt = jnp.stack(bp_l)
    new_C_sample = jnp.stack(cs_l)
    new_n_sample = jnp.stack(n_s_l)
    new_m_sample = jnp.stack(ms_l)
    new_conv_sample = jnp.stack(bs_l)
    return (xp, xs, new_k_prompt, new_v_prompt, new_k_sample, new_v_sample,
            new_C_prompt, new_n_prompt, new_m_prompt, new_conv_prompt,
            new_C_sample, new_n_sample, new_m_sample, new_conv_sample)


_drawn_inputs = setup_inputs


def setup_inputs(seed=0):
    import zlib

    import numpy as np

    out = dict(_drawn_inputs(seed))
    spreads = {}
    factors = {'att_qnorm_g': 7.507,
     'att_knorm_g': 2.824,
     'mlstm_norm_g': 2.905,
     'norm2_g': 3.147,
     'peer_qnorm_g': 3.573}
    for name, (base, spread) in spreads.items():
        noise = np.random.default_rng([zlib.crc32(name.encode()), seed]).standard_normal(out[name].shape)
        drawn = base * np.exp(spread * noise) if base else spread * noise
        out[name] = jnp.asarray(drawn.astype(out[name].dtype))
    for name, factor in factors.items():
        out[name] = (out[name] * factor).astype(out[name].dtype)
    return out
```

```python
import math

import concourse.bass as bass
from concourse import mybir

F32 = mybir.dt.float32
BF16 = mybir.dt.bfloat16
U32 = mybir.dt.uint32
ALU = mybir.AluOpType
ACT = mybir.ActivationFunctionType
AX = mybir.AxisListType

P = 128
D = 1024
KT = D // P
SEQ = 512
DB = 8
NT = SEQ + DB
HALF = NT // 2
NPT = SEQ // P
NTT = NPT + 1
H = 8
DH = 64
WID = H * DH
CW = 4
TOPK = 16
NKEYS = 128
EPS = 1e-6
NEG = -1e30
LOWEST = -3.0e38
NCACHE = 2048
DIL = ((128, 1), (512, 4), (2048, 16))
GC = 4
NG = NKEYS // GC
TB = 40
NBLK = NT // TB
QUADS = TB // 4
RING = 6

C_IDENT, C_IOTA, C_MASK, C_CAUSAL, C_COS, C_SIN, C_SEL, C_END = 0, 128, 256, 768, 896, 1056, 1216, 1224
P_G1, P_G2, P_GQN, P_CW, P_CB, P_GQ, P_GK, P_GM, P_BG8, P_M0, P_N0, P_END = (
    0, 8, 16, 18, 50, 58, 122, 186, 698, 700, 701, 768)

WGROUPS = ["mqk0", "mqk1", "q", "k", "v", "mv", "mo", "wo0", "wo1", "wq0", "wq1", "wq2", "wq3"]


def rows(i):
    return P if i < NPT else DB


def psum_plan():
    u = [("n1", f) for f in range(2)]
    u += [(g, f) for g in ("gi", "gf") for f in range(2)]
    u += [("mqk", c, f) for c in range(8) for f in range(2)]
    u += [(g, i) for g in ("q", "k", "v", "mv", "mo") for i in range(NTT)]
    u += [(g, i) for i in range(NPT) for g in ("qT", "kT")]
    att = [(i, h) for i in range(NPT) for h in range(H)]
    u += [("S", 0, 0)]
    for n, (i, h) in enumerate(att):
        if n + 1 < len(att):
            u += [("S", *att[n + 1])]
        u += [("PT", i, h)]
    u += [("aT",)] + [("kt", i) for i in range(NPT)] + [("sq",), ("sk",)]
    u += [("nM", 0)]
    for h in range(H):
        if h + 1 < H:
            u += [("nM", h + 1)]
        u += [("ST", h, j) for j in range(NPT)] + [("num", h), ("C", h)]
    u += [("qb", b) for b in range(DB)] + [("sS",), ("sP",)]
    u += [("mA", i) for i in range(NPT)] + [("mM", i) for i in range(NTT)]
    u += [("wo", m, f) for m in range(8) for f in range(2)]
    u += [("n2", f) for f in range(2)]
    u += [("wq", m, f) for m in (0, 1) for f in range(2)]
    for h in range(H):
        if h + 1 < H:
            u += [("wq", m, f) for m in (2 * h + 2, 2 * h + 3) for f in range(2)]
        u += [("sc", h, i) for i in range(NTT)]
    u += [("tb", i) for i in range(NTT)]
    return {key: n for n, key in enumerate(u)}


def trunk_and_peer(nc, I, O):
    sem = nc.alloc_semaphore
    place = psum_plan()
    full = [sem(f"psum_full{k}") for k in range(RING)]
    free = [sem(f"psum_free{k}") for k in range(RING)]
    pa = nc.alloc_psum_tensor("psum", [P, 8, 512], F32)
    bank = [pa[:, k, :] for k in range(RING)]
    acc = [pa[:, RING + k, :] for k in range(2)]

    def bank_of(key):
        return bank[place[key] % RING]

    def claim(eng, key):
        n = place[key]
        if n >= RING:
            eng.wait_ge(free[n % RING], n // RING)
        return bank[n % RING]

    def made(ins, key):
        ins.then_inc(full[place[key] % RING], 1)

    def arrived(eng, key):
        n = place[key]
        eng.wait_ge(full[n % RING], n // RING + 1)
        return bank[n % RING]

    def release(ins, key):
        ins.then_inc(free[place[key] % RING], 1)

    def emptied(eng, key):
        n = place[key]
        eng.wait_ge(free[n % RING], n // RING + 1)

    base = (nc.sbuf_base + 63) // 64 * 64

    def put(name, shape, dt, off):
        return nc.alloc_sbuf_tensor_at(name, shape, dt, offset=off)

    HT = KT * NT * 4
    a0 = base
    xT = put("xT", [P, KT, NT], F32, a0)
    hs0 = a0 + HT
    h_hi = put("h_hi", [P, KT, NT], BF16, hs0)
    h_lo = put("h_lo", [P, KT, NT], BF16, hs0 + HT // 2)
    ig, fx, lf, ax, lfm, cumB, nrow, mrow = [put(n, [H, NT], F32, hs0 + 2080 * k) for k, n in enumerate(
        ["ig", "fx", "lf", "ax", "lfm", "cumB", "nrow", "mrow"])]
    c0 = hs0 + HT
    tables = put("tables", [P, 4, NT], F32, c0)
    ones_row = put("ones_row", [H, SEQ], F32, c0)
    arow = put("arow", [H, SEQ], F32, c0 + 2048)
    enm = put("enm", [H, SEQ], F32, c0 + 4096)
    k0 = c0 + 4 * NT * 4
    const = put("const", [P, C_END], F32, k0)
    par = put("par", [P, P_END], F32, k0 + C_END * 4)
    sel = put("sel", [H, H, P], F32, k0 + (C_END + P_END) * 4)
    ones = put("ones", [P, P], F32, k0 + (C_END + P_END + 1024) * 4)
    iota_b = put("iota_b", [P, P], BF16, k0 + (C_END + P_END + 1024 + 128) * 4)
    st = put("stats", [P, 320], F32, k0 + (C_END + P_END + 1024 + 128 + 64) * 4)
    e0 = k0 + (C_END + P_END + 1024 + 128 + 64 + 320) * 4
    ident = const[:, C_IDENT:C_IDENT + P]
    iota = const[:, C_IOTA:C_IOTA + P]
    maskt = const[:, C_MASK:C_MASK + SEQ]
    causal = const[:, C_CAUSAL:C_CAUSAL + P]
    cosT = const[:, C_COS:C_SIN].rearrange("p (i r) -> p i r", r=32)
    sinT = const[:, C_SIN:C_SEL].rearrange("p (i r) -> p i r", r=32)
    seld = const[0:64, C_SEL:C_END]

    B0 = e0
    hT = put("hT", [P, KT, NT], F32, B0)
    qT = put("qT", [P, 4, SEQ], F32, B0)
    kT = put("kT", [P, 4, SEQ], F32, B0 + 8192)
    C0 = B0 + HT
    sqT = put("sqT", [P, KT, NT], F32, C0)
    mqkT = put("mqkT", [P, KT, NT], F32, C0)
    hraw = put("hraw", [P, NTT, WID], F32, C0)
    dm = put("dm", [P, NPT, P], F32, C0 + 10240)
    ht = put("ht", [P, WID], F32, C0 + 12288)
    SS = put("SS", [64, 385], F32, C0 + 14336)
    qg = [put(f"qg{b}", [P, 2, NT], F32, C0 + 4160 * b) for b in range(2)]
    qsq = [put(f"qsq{b}", [P, 2, NT], F32, C0 + 8320 + 4160 * b) for b in range(2)]
    D0 = C0 + HT
    qkT = put("qkT", [P, KT, NT], F32, D0)
    mixT = put("mixT", [P, KT, NT], F32, D0)
    E0 = D0 + HT
    zq = put("zq", [P, NTT, WID], F32, E0)
    zk = put("zk", [P, NTT, WID], F32, E0 + 10240)
    atok = put("atok", [P, NPT, WID], F32, E0)
    ktok = put("ktok", [P, NPT, WID], F32, E0 + 10240)
    F0 = E0 + 20480
    zv = put("zv", [P, NTT, WID], F32, F0)
    qks = put("qks", [DB, 2 * WID], F32, F0)
    Cst = put("Cst", [DH + 1, H, DH], F32, F0 + 4096)
    PTs = put("PTs", [P, 192], F32, F0 + 6144)
    Pd = put("Pd", [DB, 64], F32, F0 + 6912)
    sSc = put("sSc", [P, 3, DB, H], F32, F0 + 7168)
    dP = put("dP", [64, 64], F32, F0 + 7936)
    sgo = put("sgo", [P, NTT, WID], F32, F0 + 10240)
    skT = put("skT", [P, 2 * H, P], F32, F0 + 10240)
    mv1 = put("mv1", [P, NTT, H, DH + 1], F32, F0 + 20480)
    eq = put("eq", [P, P, TOPK], F32, F0 + 20480)
    G0 = F0 + 20480 + 10400
    Sb = [put(f"Sb{b}", [P, SEQ], F32, G0 + 2048 * b) for b in range(2)]
    Pb = [put(f"Pb{b}", [P, SEQ], F32, G0 + 4096 + 2048 * b) for b in range(2)]
    PTb = [put(f"PTb{b}", [P, NPT, P], F32, G0 + 8192 + 2048 * b) for b in range(2)]
    rt = put("rt", [P, WID], F32, G0 + 12288)
    rt2 = put("rt2", [P, WID], F32, G0 + 14336)
    rstd = put("rstd", [P, NT], F32, G0 + 16384)
    msq, mtmp = [put(n, [P, NT], F32, G0 + 8192 + 2080 * k) for k, n in enumerate(["msq", "mtmp"])]
    OJ = [0, 512, 896, 1152]
    Dm = [put(f"Dm{b}", [P, 1280], F32, G0 + 5120 * b) for b in range(2)]
    sdm = [put(f"sdm{b}", [P, 1280], F32, G0 + 10240 + 5120 * b) for b in range(2)]
    Cs = put("Cs", [P, 32, DH], F32, G0)
    Ct = put("Ct", [P, 32, DH], F32, G0 + 8192)
    kprod = put("kprod", [P, 3, WID], F32, G0 + 8192)
    sml = put("sml", [P, 512], F32, G0 + 16384)
    rstd2 = put("rstd2", [P, NT], F32, G0)
    W0 = G0 + 20480
    wr = [put(f"wr{b}", [P, KT, 512], F32, W0 + 16384 * b) for b in range(2)]
    NKV = 5
    kv = [put(f"kv{b}", [P, 3, WID], F32, W0 + 6144 * b) for b in range(NKV)]
    X0 = W0 + 32768
    wg = put("wg", [P, KT, 16], F32, X0)
    cst = put("cst", [P, KT, 3, DB], F32, X0 + 512)
    convt = put("convt", [P, KT, 3, DB], F32, X0 + 1280)
    wk = [put(f"wk{b}", [P, NPT, DH], F32, X0 + 1024 * b) for b in range(2)]
    assert X0 + 2048 <= nc.sbuf_usable_end, (X0 + 2048 - nc.sbuf_usable_end)
    vals = put("vals", [P, 2, TOPK], F32, E0)
    ixs = put("ixs", [P, 2, TOPK], U32, E0 + 128)
    Ssb = put("Ssb", [P, 2, P], F32, E0 + 256)
    Srep = put("Srep", [P, 256], F32, E0 + 1280)
    cand = put("cand", [P, TOPK, TOPK], F32, E0 + 2304)
    SC = put("SC", [P, NTT, P], F32, E0 + 3328)
    CI = put("CI", [P, NTT, P], U32, E0 + 5888)
    I1 = put("I1", [P, NTT, P], F32, E0 + 8448)
    I2 = put("I2", [P, NTT, P], F32, E0 + 11008)
    idx = put("idx", [P, 2, P], F32, E0 + 13568)
    gt = put("gt", [P, P], F32, E0 + 14592)
    abu = put("abu", [P, 2, P], U32, E0 + 15104)
    abf = put("abf", [P, 2, P], F32, E0 + 16128)
    ghb = put("ghb", [P, P], BF16, E0 + 17152)

    L0 = c0
    u_raw = [put(f"u_raw{b}", [P, KT, GC * P], F32, L0 + 16384 * b) for b in range(2)]
    L1 = L0 + 32768
    u_hi = [put(f"u_hi{b}", [P, KT, GC * P], BF16, L1 + 16384 * b) for b in range(2)]
    u_lo = [put(f"u_lo{b}", [P, KT, GC * P], BF16, L1 + 8192 + 16384 * b) for b in range(2)]
    L2 = L1 + 32768
    v_raw = [put(f"v_raw{b}", [P, GC, D], F32, L2 + 16384 * b) for b in range(2)]
    L3 = L2 + 32768
    v_hi = [put(f"v_hi{b}", [P, GC, D], BF16, L3 + 16384 * b) for b in range(2)]
    v_lo = [put(f"v_lo{b}", [P, GC, D], BF16, L3 + 8192 + 16384 * b) for b in range(2)]
    L4 = L3 + 32768
    g_in = [put(f"g_in{b}", [P, NBLK, GC, TB], F32, L4 + 8320 * b) for b in range(2)]
    L5 = L4 + 16640
    w_hi = [put(f"w_hi{b}", [P, GC, NT], BF16, L5 + 8320 * b) for b in range(2)]
    w_lo = [put(f"w_lo{b}", [P, GC, NT], BF16, L5 + 4160 + 8320 * b) for b in range(2)]
    L6 = L5 + 16640
    act_f = [put(f"act_f{b}", [P, NT], F32, L6 + 2080 * b) for b in range(2)]
    w_f = [put(f"w_f{b}", [P, NT], F32, L6 + 4160 + 2080 * b) for b in range(2)]
    assert L6 + 8320 <= nc.sbuf_usable_end, (L6 + 8320 - nc.sbuf_usable_end)
    T0 = e0
    stage = [put(f"stage{b}", [P, NKEYS, TB], F32, T0 + 20480 * b) for b in range(2)]
    T1 = T0 + 40960
    oneR = [put(f"oneR{b}", [P, 4, P], BF16, T1 + 1024 * b) for b in range(5)]
    T2 = T1 + 5120
    gateL = [put(f"gateL{b}", [P, 4, 2, P], BF16, T2 + 2048 * b) for b in range(5)]
    T3 = T2 + 10240
    cur = [put(f"cur{b}", [P, 4, TB], F32, T3 + 640 * b) for b in range(2)]
    gbank = bank[0:5]
    abank = [pa[:, 2 * b:2 * b + 2, :] for b in range(2)]
    bbank = [pa[:, 4 + 2 * b:6 + 2 * b, :] for b in range(2)]

    d_qk = nc.dram_tensor("d_qk", (2, DB, WID), F32).ap()
    d_v = nc.dram_tensor("d_v", (DB, WID), F32).ap()
    d_g = nc.dram_tensor("d_g", (2, DB, H), F32).ap()
    d_new = nc.dram_tensor("d_new", (DB, H), F32).ap()
    d_h = nc.dram_tensor("d_h", (P, 32), F32).ap()
    d_gate = nc.dram_tensor("d_gate", (NBLK, P, NKEYS, TB), F32).ap()

    def sems(names):
        return [sem(n) for n in names.split()]

    x_in = [sem(f"x_in{k}") for k in range(KT)]
    const_in, sel_in, wg_in, cst_in, sk_in = sems("const_in sel_in wg_in cst_in sk_in")
    w_in = [sem(f"w_in{b}") for b in range(2)]
    kv_in = [sem(f"kv_in{b}") for b in range(NKV)]
    dve, act_o, pool_turn = sems("dve_order act_order pool_turn")
    ones_set, sq_done, h_done, ax_done, ln_done, lf_done, m_done, enm_done = sems(
        "ones_set sq_done h_done ax_done ln_done lf_done m_done enm_done")
    conv_done, silu_done, kscaled, conv_out = sems("conv_done silu_done kscaled conv_out")
    rope_done, new_done, kp_out, vp_out, m_out = sems("rope_done new_done kp_out vp_out m_out")
    att_scored, att_exp, att_pv, att_out = sems("att_scored att_exp att_pv att_out")
    ml_diag, ml_exp, ml_wk, ml_norm = sems("ml_diag ml_exp ml_wk ml_norm")
    scr_g, scr_qk, scr_v, scr_new, scr_h = sems("scr_g scr_qk scr_v scr_new scr_h")
    sml_in, ss_in, h4_in, c_in = sems("sml_in ss_in h4_in c_in")
    k_used, s_neg, s_exp, s_prob, v_used, s_mixed = sems("k_used s_neg s_exp s_prob v_used s_mixed")
    ms_ready, ms_exp, ms_h, ms_C, ms_out, Cp_out = sems("ms_ready ms_exp ms_h ms_C ms_out Cp_out")
    sq2_done, h2_done, hs_done = sems("sq2_done h2_done hs_done")
    g_sub, g_exp, tb_done, tb_ready = sems("g_sub g_exp tb_done tb_ready")
    cur_done, gl_L, gl_R, gl_mm, gl_ev = sems("cur_done gl_L gl_R gl_mm gl_ev")
    g_stored = [sem(f"g_stored{b}") for b in range(2)]
    u_in, v_in, gg_in = ([sem(f"{n}{b}") for b in range(2)] for n in ("u_in", "v_in", "gg_in"))
    uhi_done, ulo_done, vhi_done, vlo_done = sems("uhi_done ulo_done vhi_done vlo_done")
    a_made, a_gelu, w_prod, whi_done, wlo_done, b_made, b_added = sems(
        "a_made a_gelu w_prod whi_done wlo_done b_made b_added")
    y_out = sem("y_out")
    CONV_OUT, KP_OUT, VP_OUT, MS_OUT, CP_OUT, SML_IN = 3 * 16, (NPT + 1) * 16, (NPT + 1) * 16, 3 * 16, 2 * 16, 9 * 16

    class Ordered:

        def __init__(self, eng, order):
            self.eng, self.order, self.count = eng, order, {}

        def __call__(self, ins, signal=None):
            s = signal or self.order
            self.count[s.name] = self.count.get(s.name, 0) + 1
            ins.then_inc(s, 1)
            self.eng.wait_ge(s, self.count[s.name])

        def release(self, ins, key):
            release(ins, key)
            emptied(self.eng, key)

    class Group:

        def __init__(self, i, b):
            self.i, self.b, self.n = i + b // 2, b % 2, (i + b // 2) * 2 + b % 2

        def plus(self, k):
            return Group(self.i, self.b + k)

    def wait_pos(eng, s, v):
        if not isinstance(v, int) or v > 0:
            eng.wait_ge(s, v)

    def groups(eng, step):
        for b in range(2):
            step(Group(0, b), False)
        with eng.Fori(1, NG // 2 - 1) as i:
            for b in range(2):
                step(Group(i, b), False)
        for b in range(2):
            step(Group(NG // 2 - 1, b), True)

    def blocks(eng, step):
        step(0, 0, 0)
        step(1, 1, 0)
        step(2, 0, 1)
        with eng.Fori(1, (NBLK - 1) // 2) as i:
            step(i * 2 + 1, 1, i)
            step(i * 2 + 2, 0, i + 1)

    ATT = [(i, h) for i in range(NPT) for h in range(H)]
    LASTS = {"mqk0": ("mqk", 3, 1), "mqk1": ("mqk", 7, 1), "wo0": ("wo", 3, 1), "wo1": ("wo", 7, 1)}
    LASTS.update({g: (g, NTT - 1) for g in ("q", "k", "v", "mv", "mo")})
    LASTS.update({f"wq{g}": ("wq", 4 * g + 3, 1) for g in range(4)})

    def weights_arrived(eng, group):
        n = WGROUPS.index(group)
        eng.wait_ge(w_in[n % 2], 16 * (n // 2 + 1))
        return wr[n % 2]

    block = nc.Block()
    with nc.allow_non_contiguous_dma(reason="a few hundred small elements of the decode batch"), block as blk:

        @blk.sync
        def _(sp):
            sp.dma_start(const[:, :], I["const"]).then_inc(const_in, 16)
            sp.dma_start(par[:, :], I["par"]).then_inc(const_in, 16)
            for k in range(KT):
                sp.dma_start(xT[:, k, :], I["xT"][:, k, :]).then_inc(x_in[k], 16)
            sp.dma_start(wg[:, :, :], I["wg"]).then_inc(wg_in, 16)
            for n, g in enumerate(WGROUPS):
                if n == 7:
                    arrived(sp, ("mo", NTT - 1))
                    emptied(sp, ("mo", NTT - 1))
                    for m in range(2 * DB):
                        b, cache = m % DB, I["ck"] if m < DB else I["cv"]
                        if m >= NKV:
                            if m - NKV < DB:
                                sp.wait_ge(k_used, m - NKV + 1)
                            else:
                                sp.wait_ge(v_used, m - NKV - DB + 1)
                        for g3, (_, dil) in enumerate(DIL):
                            sp.dma_start(kv[m % NKV][:, g3, :],
                                         cache[b, NCACHE - P * dil:NCACHE:dil, :]).then_inc(kv_in[m % NKV], 16)
                    sp.wait_ge(v_used, DB)
                    sp.dma_start(wr[n % 2][:, :, :], I["w"][n]).then_inc(w_in[n % 2], 16)
                    continue
                if n >= 2 and n != 8:
                    arrived(sp, LASTS[WGROUPS[n - 2]])
                sp.dma_start(wr[n % 2][:, :, :], I["w"][n]).then_inc(w_in[n % 2], 16)
                if n == 9:
                    sp.dma_start(skT[:, :, :], I["sk"]).then_inc(sk_in, 16)
            def store(n, b, i):
                sp.wait_ge(gl_ev, (n + 1) * QUADS)
                sp.dma_start(d_gate[bass.ds(n, 1)].rearrange("a p e t -> p (a e t)"),
                             stage[b][:, :, :].rearrange("p e t -> p (e t)")).then_inc(g_stored[b], 16)

            blocks(sp, store)
            sp.wait_ge(g_stored[0], 16 * (NBLK // 2 + 1))
            sp.wait_ge(g_stored[1], 16 * (NBLK // 2))

            def load(g):
                n, b = g.n, g.b
                wait_pos(sp, ulo_done, (n - 1) * 4)
                sp.dma_start(u_raw[b][:, :, :].rearrange("p k e -> p (k e)"),
                             I["uT"][bass.ds(n, 1)].rearrange("a p e -> p (a e)")).then_inc(u_in[b], 16)
                wait_pos(sp, w_prod, (n - 1) * GC)
                sp.dma_start(g_in[b][:, :, :, :],
                             d_gate[:, :, bass.ds(n * GC, GC), :].rearrange("a p e t -> p a e t")
                             ).then_inc(gg_in[b], 16)
                wait_pos(sp, vlo_done, (n - 1) * 4)
                sp.dma_start(v_raw[b][:, :, :].rearrange("p k e -> p (k e)"),
                             I["v"][bass.ds(n, 1)].rearrange("a p e -> p (a e)")).then_inc(v_in[b], 16)

            groups(sp, lambda g, last: load(g))
            for m in range(KT):
                sp.wait_ge(b_added, (NG - 1) * KT + m + 1)
                sp.dma_start(O["yT"][:, m, :], xT[:, m, :]).then_inc(y_out, 16)
            sp.wait_ge(y_out, 16 * KT)

        @blk.gpsimd
        def _(pool):
            pool.dma_start(sel[:, :, :], I["sel"]).then_inc(sel_in, 16)
            pool.dma_start(cst[:, :, :, :], I["cst"]).then_inc(cst_in, 16)
            pool.wait_ge(cst_in, 16)
            pool.dma_start(O["convs"][:, :, 0:2, :], cst[:, :, 1:3, :]).then_inc(conv_out, 16)
            for c in range(8):
                for f in range(2):
                    emptied(pool, ("mqk", c, f))
            pool.dma_start(O["convs"][:, :, 2, :], mqkT[:, :, SEQ:NT]).then_inc(conv_out, 16)
            pool.dma_start(O["convp"], mqkT[:, :, SEQ - 3:SEQ]).then_inc(conv_out, 16)
            pool.wait_ge(lf_done, 1)
            pool.dma_start(d_g[0].rearrange("b h -> h b"), ig[:, SEQ:NT]).then_inc(scr_g, 16)
            pool.dma_start(d_g[1].rearrange("b h -> h b"), lf[:, SEQ:NT]).then_inc(scr_g, 16)
            pool.wait_ge(m_done, 1)
            pool.dma_start(O["mp"], mrow[:, SEQ - 1:SEQ]).then_inc(m_out, 16)
            for i in range(NTT):
                emptied(pool, ("v", i))
            for i in range(NPT):
                pool.dma_start(O["vp"][i], zv[:, i, :]).then_inc(vp_out, 16)
            pool.dma_start(O["vs"], zv[0:DB, NPT, :]).then_inc(vp_out, 16)
            emptied(pool, ("mv", NTT - 1))
            pool.dma_start(d_v.rearrange("b (h d) -> b h d", h=H), mv1[0:DB, NPT, :, 0:DH]).then_inc(scr_v, 16)
            pool.wait_ge(rope_done, 2 * NTT)
            for i in range(NPT):
                pool.dma_start(O["kp"][i], zk[:, i, :]).then_inc(kp_out, 16)
            pool.dma_start(O["ks"], zk[0:DB, NPT, :]).then_inc(kp_out, 16)
            pool.wait_ge(new_done, 1)
            pool.dma_start(d_new, st[0:DB, 184:192]).then_inc(scr_new, 16)
            pool.wait_ge(scr_new, 16)
            pool.wait_ge(conv_done, 8)
            pool.wait_ge(conv_out, CONV_OUT)
            pool.dma_start(SS[:, 384:385], d_new.rearrange("b (h o) -> (b h) o", o=1)).then_inc(ss_in, 16)
            emptied(pool, ("sq",))
            emptied(pool, ("sk",))
            for t in range(2):
                pool.dma_start(d_qk[t], qks[:, t * WID:(t + 1) * WID]).then_inc(scr_qk, 16)
            pool.wait_ge(scr_g, 32)
            pool.wait_ge(scr_v, 16)
            pool.wait_ge(scr_qk, 32)
            for h in (H - 2, H - 1):
                arrived(pool, ("num", h))
                for j in range(NPT):
                    emptied(pool, ("ST", h, j))
            pool.wait_ge(ml_wk, NPT * H)
            pool.dma_start(Cs[:, :, :], I["C0"]).then_inc(c_in, 16)
            for half in range(2):
                for t in range(2):
                    pool.dma_start(sml[half:P:2, t * DH:(t + 1) * DH],
                                   d_qk[t].rearrange("b (h d) -> (b h) d", h=H)).then_inc(sml_in, 16)
                for t in range(2):
                    pool.dma_start(sml[half:P:2, 160 + t:161 + t],
                                   d_g[t].rearrange("b (h o) -> (b h) o", o=1)).then_inc(sml_in, 16)
            pool.dma_start(sml[:, 128:160], d_v.rearrange("b (x v) -> (b x) v", v=32)).then_inc(sml_in, 16)
            for h in range(H):
                emptied(pool, ("C", h))
            pool.dma_start(O["Cp"].rearrange("h v k -> v h k"), Cst[0:DH, :, :]).then_inc(Cp_out, 16)
            pool.dma_start(O["np"], Cst[DH:DH + 1, :, :]).then_inc(Cp_out, 16)
            pool.wait_ge(ms_h, 1)
            pool.dma_start(d_h, sml[:, 170:202]).then_inc(scr_h, 16)
            pool.wait_ge(scr_h, 16)
            pool.dma_start(hraw[0:DB, NPT, :], d_h.rearrange("(b x) v -> b x v", b=DB)).then_inc(h4_in, 16)
            pool.wait_ge(ms_C, 1)
            pool.dma_start(O["Cs"], Cs[:, :, :]).then_inc(ms_out, 16)
            pool.dma_start(O["ns"], sml[0:P:2, 256:320]).then_inc(ms_out, 16)
            pool.dma_start(O["ms"], sml[0:P:2, 320:321]).then_inc(ms_out, 16)
            for s, v in ((m_out, 16), (vp_out, VP_OUT), (kp_out, KP_OUT), (Cp_out, CP_OUT), (ms_out, MS_OUT)):
                pool.wait_ge(s, v)

            def one_hot(n, b, i):
                pool.wait_ge(cur_done, n + 1)
                for q in range(QUADS):
                    slot = q % 5
                    wait_pos(pool, gl_mm, n * QUADS + (q - 4))
                    pool.sem_inc(pool_turn, 1)
                    for t in range(4):
                        ins = pool.tensor_scalar(oneR[slot][:, t, :], iota_b[:, :],
                                                 cur[b][:, 1, 4 * q + t:4 * q + t + 1], None, ALU.is_equal)
                    ins.then_inc(gl_R, 1)

            blocks(pool, one_hot)

        @blk.scalar
        def _(act):
            A = act.activation

            def copy(key, dst, src):
                release(A(dst, src, ACT.Copy), key)

            for c in range(8):
                for f in range(2):
                    bk = arrived(act, ("mqk", c, f))
                    copy(("mqk", c, f), mqkT[:, c, f * HALF:(f + 1) * HALF], bk[:, 0:HALF])
            act.wait_ge(ax_done, 1)
            A(lfm[:, :], ax[:, :], ACT.Exp, scale=-1.0).then_inc(act_o, 1)
            act.wait_ge(act_o, 1)
            A(lfm[:, :], lfm[:, :], ACT.Ln, bias=1.0).then_inc(ln_done, 1)
            for g, dst in (("q", zq), ("k", zk), ("v", zv)):
                for i in range(NTT):
                    bk = arrived(act, (g, i))
                    copy((g, i), dst[0:rows(i), i, :], bk[0:rows(i), :])
            for i in range(NTT):
                bk = arrived(act, ("mv", i))
                copy(("mv", i), mv1[0:rows(i), i, :, 0:DH], bk[0:rows(i), :].rearrange("p (h d) -> p h d", h=H))
            for i in range(NTT):
                bk = arrived(act, ("mo", i))
                release(A(sgo[0:rows(i), i, :], bk[0:rows(i), :], ACT.Sigmoid), ("mo", i))
            for c in range(8):
                act.wait_ge(conv_done, c + 1)
                A(qkT[:, c, :], qkT[:, c, :], ACT.Silu).then_inc(silu_done, 1)
            act.wait_ge(m_done, 1)
            A(enm[:, :], mrow[:, 0:SEQ], ACT.Exp, scale=-1.0).then_inc(enm_done, 1)
            arrived(act, ("mo", NTT - 1))
            for i in range(NPT):
                for g, dst in (("qT", qT), ("kT", kT)):
                    bk = arrived(act, (g, i))
                    copy((g, i), dst[:, :, i * P:(i + 1) * P], bk[:, :].rearrange("p (c t) -> p c t", c=4))
            for n, (i, h) in enumerate(ATT):
                act.wait_ge(att_scored, n + 1)
                if n >= 2:
                    arrived(act, ("PT", *ATT[n - 2]))
                if h == 0 and i >= 2:
                    act.wait_ge(att_out, i - 1)
                A(Pb[n % 2][:, 0:(i + 1) * P], Sb[n % 2][:, 0:(i + 1) * P], ACT.Exp,
                  bias=st[:, 18 + n % 2:19 + n % 2],
                  accum_out=st[:, 20 + 8 * (i % 2) + h:21 + 8 * (i % 2) + h]).then_inc(att_exp, 1)
            bk = arrived(act, ("aT",))
            copy(("aT",), st[:, 48:112], bk[:, 0:64])
            act.wait_ge(kp_out, KP_OUT)
            for i in range(NPT):
                bk = arrived(act, ("kt", i))
                copy(("kt", i), ktok[:, i, :], bk[:, :])
            act.wait_ge(vp_out, VP_OUT)
            act.wait_ge(att_pv, len(ATT))
            for n, key in enumerate((("sq",), ("sk",))):
                bk = arrived(act, key)
                copy(key, qks[:, n * WID:(n + 1) * WID], bk[0:DB, :])

            def decay(h):
                b = h % 2
                bk = arrived(act, ("nM", h))
                act.wait_ge(ml_diag, h + 1)
                if h >= 2:
                    act.wait_ge(ml_wk, NPT * (h - 1))
                for j in range(NPT - 1):
                    ins = A(Dm[b][:, OJ[j] + P:OJ[j] + (NPT - j) * P], bk[:, (j + 1) * P:SEQ], ACT.Exp,
                            bias=st[:, 48 + j * H + h:49 + j * H + h])
                    if j == NPT - 2:
                        release(ins, ("nM", h))
                for j in range(NPT):
                    ins = A(Dm[b][:, OJ[j]:OJ[j] + P], dm[:, j, :], ACT.Exp,
                            bias=st[:, 48 + j * H + h:49 + j * H + h])
                ins.then_inc(ml_exp, 1)

            emptied(act, ("aT",))
            act.wait_ge(att_out, NPT)
            decay(0)
            for h in range(H):
                if h + 1 < H:
                    decay(h + 1)
                bk = arrived(act, ("C", h))
                copy(("C", h), Cst[:, h, :], bk[0:DH + 1, 0:DH])
            act.wait_ge(s_neg, 1)
            A(SS[:, :], SS[:, :], ACT.Exp, bias=st[0:64, 141:142], accum_out=st[0:64, 142:143]).then_inc(s_exp, 1)
            act.wait_ge(ms_ready, 1)
            A(sml[:, 166:169], sml[:, 163:166], ACT.Exp).then_inc(ms_exp, 1)
            for i in range(NPT):
                bk = arrived(act, ("mA", i))
                copy(("mA", i), mixT[:, 0:4, i * P:(i + 1) * P], bk[:, :].rearrange("p (c t) -> p c t", c=4))
            for i in range(NTT):
                r = rows(i)
                bk = arrived(act, ("mM", i))
                copy(("mM", i), mixT[:, 4:8, i * P:i * P + r],
                     bk[:, 0:4 * r].rearrange("p (c t) -> p c t", c=4))
            for h in range(H):
                for m in (2 * h, 2 * h + 1):
                    for f in range(2):
                        bk = arrived(act, ("wq", m, f))
                        if h >= 2:
                            arrived(act, ("sc", h - 2, NTT - 1))
                        A(qg[h % 2][:, m % 2, f * HALF:(f + 1) * HALF], bk[:, 0:HALF], ACT.Identity,
                          scale=par[:, P_GQN + m % 2:P_GQN + m % 2 + 1]).then_inc(act_o, 1)
                        release(A(qsq[h % 2][:, m % 2, f * HALF:(f + 1) * HALF], bk[:, 0:HALF], ACT.Square),
                                ("wq", m, f))
            for i in range(NTT):
                act.wait_ge(g_sub, i + 1)
                A(gt[0:rows(i), :], gt[0:rows(i), :], ACT.Exp).then_inc(g_exp, 1)

            def evacuate(n, b, i):
                wait_pos(act, g_stored[b], 16 * i)
                for q in range(QUADS):
                    act.wait_ge(gl_mm, n * QUADS + q + 1)
                    A(stage[b][:, :, 4 * q:4 * q + 4],
                      gbank[q % 5][:, :].rearrange("p (t e) -> p e t", t=4), ACT.Copy).then_inc(gl_ev, 1)

            blocks(act, evacuate)

            def u_high(g):
                act.wait_ge(u_in[g.b], (g.i + 1) * 16)
                wait_pos(act, a_made, (g.n - 1) * GC)
                for s in range(4):
                    A(u_hi[g.b][:, 2 * s:2 * s + 2, :], u_raw[g.b][:, 2 * s:2 * s + 2, :], ACT.Copy
                      ).then_inc(uhi_done, 1)

            def v_high(g):
                act.wait_ge(v_in[g.b], (g.i + 1) * 16)
                wait_pos(act, b_made, (g.n - 1) * KT)
                for s in range(4):
                    A(v_hi[g.b][:, s, :], v_raw[g.b][:, s, :], ACT.Copy).then_inc(vhi_done, 1)

            def gelu(g):
                for c in range(GC):
                    u = g.n * GC + c
                    act.wait_ge(a_made, u + 1)
                    wait_pos(act, w_prod, u - 1)
                    A(act_f[c % 2][:, :].rearrange("p (f t) -> p f t", f=2), abank[c % 2][:, :, 0:HALF], ACT.Gelu
                      ).then_inc(a_gelu, 1)

            def act_step(g, last):
                more = not (last and g.b == 1)
                if more:
                    gelu(g.plus(1))
                if not last:
                    u_high(g.plus(2))
                if more:
                    v_high(g.plus(1))

            act.wait_ge(gl_ev, NBLK * QUADS)
            first = Group(0, 0)
            u_high(first)
            u_high(first.plus(1))
            v_high(first)
            gelu(first)
            groups(act, act_step)

        @blk.vector
        def _(v):
            do = Ordered(v, dve)
            tt, ts, stt = v.tensor_tensor, v.tensor_scalar, v.scalar_tensor_tensor

            def inv_sqrt(y, x, t):
                do(ts(t.bitcast(U32), x.bitcast(U32), 1, None, ALU.logical_shift_right))
                do(ts(y.bitcast(U32), t.bitcast(U32), -1.0, float(0x5F3759DF), ALU.mult, ALU.add))
                for _ in range(3):
                    do(tt(t, y, y, ALU.mult))
                    do(stt(t, t, -0.5, x, ALU.mult, ALU.mult))
                    do(stt(y, t, 1.5, y, ALU.add, ALU.mult))

            nv, na, ny = st[:, 192:232], st[:, 232:272], st[:, 272:312]

            def head_stat(src, tmp, i):
                r = rows(i)
                do(tt(tmp[0:r, :], src, src, ALU.mult))
                do(v.tensor_reduce(nv[0:r, i * H:(i + 1) * H], tmp[0:r, :].rearrange("p (h d) -> p h d", h=H),
                                   AX.X, ALU.add))

            def inv_rms(n):
                do(ts(nv, nv, 1.0 / n, EPS, ALU.mult, ALU.add))
                inv_sqrt(ny, nv, na)

            do(v.memset(ones[:, :], 1.0), ones_set)
            do(v.memset(ones_row[:, :], 1.0))
            do(v.memset(nv, 1.0))
            for i in range(NTT):
                do(v.memset(mv1[:, i, :, DH:DH + 1], 1.0))
            v.wait_ge(const_in, 32)
            do(v.tensor_copy(iota_b[:, :], iota))
            for k in range(KT):
                v.wait_ge(x_in[k], 16)
                do(tt(sqT[:, k, :], xT[:, k, :], xT[:, k, :], ALU.mult), sq_done)
            for f in range(2):
                bk = arrived(v, ("n1", f))
                do.release(ts(msq[:, f * HALF:(f + 1) * HALF], bk[:, 0:HALF], 1.0 / D, EPS, ALU.mult, ALU.add),
                           ("n1", f))
            inv_sqrt(rstd[:, :], msq[:, :], mtmp[:, :])
            for k in range(KT):
                do(stt(hT[:, k, :], xT[:, k, :], par[:, P_G1 + k:P_G1 + k + 1], rstd[:, :], ALU.mult, ALU.mult),
                   h_done)
            for n, (g, dst) in enumerate((("gi", ig), ("gf", fx))):
                for f in range(2):
                    bk = arrived(v, (g, f))
                    do.release(ts(dst[:, f * HALF:(f + 1) * HALF], bk[0:H, 0:HALF],
                                  par[0:H, P_BG8 + n:P_BG8 + n + 1], None, ALU.add), (g, f))
            do(stt(ax[:, :], fx[:, :], -1.0, fx[:, :], ALU.mult, ALU.max), ax_done)
            do(ts(fx[:, :], fx[:, :], 0.0, None, ALU.min))
            v.wait_ge(ln_done, 1)
            do(tt(lf[:, :], fx[:, :], lfm[:, :], ALU.subtract), lf_done)
            do(v.tensor_tensor_scan(cumB[:, 0:SEQ], ones_row[:, :], lf[:, 0:SEQ], 0.0, ALU.mult, ALU.add))
            do(tt(arow[:, :], ig[:, 0:SEQ], cumB[:, 0:SEQ], ALU.subtract))
            do(v.tensor_tensor_scan(nrow[:, 0:SEQ], ones_row[:, :], arow[:, :], 0.0, ALU.mult, ALU.max))
            do(tt(mrow[:, 0:SEQ], cumB[:, 0:SEQ], nrow[:, 0:SEQ], ALU.add), m_done)
            do(ts(nrow[:, 0:SEQ], nrow[:, 0:SEQ], -1.0, None, ALU.mult))
            v.wait_ge(cst_in, 16)
            for j in range(CW - 1):
                do(tt(convt[:, :, j, :], cst[:, :, j, :],
                      par[:, P_CW:P_CW + 32].rearrange("p (c w) -> p c w", w=4)[:, :, j:j + 1].to_broadcast([P, KT, DB]),
                      ALU.mult))
            for c in range(KT):
                for f in range(2):
                    emptied(v, ("mqk", c, f))
                w = lambda j: par[:, P_CW + 4 * c + j:P_CW + 4 * c + j + 1]
                do(ts(qkT[:, c, :], mqkT[:, c, :], w(3), par[:, P_CB + c:P_CB + c + 1], ALU.mult, ALU.add))
                for j in range(CW - 1):
                    do(tt(qkT[:, c, SEQ:NT], qkT[:, c, SEQ:NT], convt[:, c, j, :], ALU.add))
                for j in (2, 1, 0):
                    s = 3 - j
                    do(stt(qkT[:, c, s:SEQ], mqkT[:, c, 0:SEQ - s], w(j), qkT[:, c, s:SEQ], ALU.mult, ALU.add),
                       conv_done if j == 0 else None)

            def rope(z, i, gain):
                r = rows(i)
                zf = z[0:r, i, :]
                z3 = zf.rearrange("p (h d) -> p h d", h=H)
                t3 = rt[0:r, :].rearrange("p (h d) -> p h d", h=H)
                u3 = rt2[0:r, :].rearrange("p (h d) -> p h d", h=H)
                ss = ny[0:r, i * H:(i + 1) * H]
                do(tt(z3, z3, ss.unsqueeze(2).to_broadcast([r, H, DH]), ALU.mult))
                do(tt(z3, z3, par[0:r, gain:gain + DH].unsqueeze(1).to_broadcast([r, H, DH]), ALU.mult))
                cos = cosT[0:r, i, :].unsqueeze(1).to_broadcast([r, H, 32])
                sin = sinT[0:r, i, :].unsqueeze(1).to_broadcast([r, H, 32])
                do(tt(t3[:, :, 0:32], z3[:, :, 0:32], cos, ALU.mult))
                do(tt(u3[:, :, 0:32], z3[:, :, 32:64], sin, ALU.mult))
                do(tt(t3[:, :, 32:64], z3[:, :, 0:32], sin, ALU.mult))
                do(tt(u3[:, :, 32:64], z3[:, :, 32:64], cos, ALU.mult))
                do(tt(z3[:, :, 0:32], t3[:, :, 0:32], u3[:, :, 0:32], ALU.subtract))
                do(tt(z3[:, :, 32:64], t3[:, :, 32:64], u3[:, :, 32:64], ALU.add), rope_done)

            for g, z, gain in (("q", zq, P_GQ), ("k", zk, P_GK)):
                for i in range(NTT):
                    emptied(v, (g, i))
                    head_stat(z[0:rows(i), i, :], rt, i)
                inv_rms(DH)
                if g == "q":
                    do(ts(ny, ny, DH ** -0.5, None, ALU.mult))
                for i in range(NTT):
                    rope(z, i, gain)
            do(tt(rt[0:DB, :], zq[0:DB, NPT, :], zk[0:DB, NPT, :], ALU.mult))
            do(v.tensor_reduce(st[0:DB, 184:192], rt[0:DB, :].rearrange("p (h d) -> p h d", h=H), AX.X, ALU.add),
               new_done)
            v.wait_ge(silu_done, 8)
            for c in range(4, 8):
                do(ts(qkT[:, c, :], qkT[:, c, :], DH ** -0.5, None, ALU.mult), kscaled)

            def score(n):
                i, h = ATT[n]
                w = (i + 1) * P
                bk = arrived(v, ("S", i, h))
                if n >= 2:
                    v.wait_ge(att_exp, n - 1)
                do.release(v.tensor_tensor_reduce(Sb[n % 2][:, 0:w], bk[:, 0:w], maskt[:, 384 - i * P:SEQ], 1.0, -3e38,
                                                  ALU.add, ALU.max, st[:, 16 + n % 2:17 + n % 2]), ("S", i, h))
                do(ts(st[:, 18 + n % 2:19 + n % 2], st[:, 16 + n % 2:17 + n % 2], -1.0, None, ALU.mult), att_scored)

            score(0)
            for n, (i, h) in enumerate(ATT):
                if n + 1 < len(ATT):
                    score(n + 1)
                w = (i + 1) * P
                bk = arrived(v, ("PT", i, h))
                if n >= 2:
                    v.wait_ge(att_pv, n - 1)
                do.release(v.tensor_copy(PTb[n % 2][:, 0:i + 1, :], bk[:, 0:w].rearrange("p (j t) -> p j t", j=i + 1)),
                           ("PT", i, h))
                if h == H - 1:
                    v.wait_ge(att_pv, n + 1)
                    l0 = 20 + 8 * (i % 2)
                    do(v.reciprocal(st[:, 36:44], st[:, l0:l0 + 8]))
                    do(tt(atok[:, i, :].rearrange("p (h d) -> p h d", h=H),
                          acc[i % 2][:, :].rearrange("p (h d) -> p h d", h=H),
                          st[:, 36:44].unsqueeze(2).to_broadcast([P, H, DH]), ALU.mult), att_out)

            v.wait_ge(conv_out, CONV_OUT)

            def diagonal(h):
                bk = arrived(v, ("nM", h))
                if h >= 1:
                    v.wait_ge(ml_exp, h)
                do(tt(dm[:, :, :], bk[:, :].rearrange("p (j t) -> p j t", j=NPT),
                      causal.unsqueeze(1).to_broadcast([P, NPT, P]), ALU.add), ml_diag)

            diagonal(0)
            for h in range(H):
                b = h % 2
                if h + 1 < H:
                    diagonal(h + 1)
                v.wait_ge(ml_exp, h + 1)
                if h >= 2:
                    arrived(v, ("num", h - 2))
                    arrived(v, ("C", h - 2))
                for j in range(NPT):
                    w = (NPT - j) * P
                    bk = arrived(v, ("ST", h, j))
                    do.release(tt(sdm[b][:, OJ[j]:OJ[j] + w], bk[:, 0:w], Dm[b][:, OJ[j]:OJ[j] + w], ALU.mult),
                               ("ST", h, j))
                for j in range(NPT):
                    last = OJ[j] + (NPT - j) * P - 1
                    if h == 0:
                        emptied(v, ("kt", j))
                    do(ts(wk[b][:, j, :], ktok[:, j, h * DH:(h + 1) * DH], Dm[b][:, last:last + 1], None, ALU.mult),
                       ml_wk)
                bk = arrived(v, ("num", h))
                num = bk[:, 0:4 * (DH + 1)].rearrange("p (i d) -> p i d", i=NPT)
                den = st[:, 112:116]
                do(v.tensor_copy(den, num[:, :, DH]))
                do(stt(den, den, -1.0, den, ALU.mult, ALU.max))
                do(tt(den, den, st[:, 80 + h:112:H], ALU.max))
                do(v.reciprocal(den, den))
                do.release(tt(hraw[:, 0:NPT, h * DH:(h + 1) * DH], num[:, :, 0:DH],
                              den.unsqueeze(2).to_broadcast([P, NPT, DH]), ALU.mult), ("num", h))

            for b in range(DB):
                bk = arrived(v, ("qb", b))
                v.wait_ge(kv_in[b % NKV], 48 * (b // NKV + 1))
                do.release(tt(kprod[:, :, :], kv[b % NKV][:, :, :],
                              bk[:, :].unsqueeze(1).to_broadcast([P, 3, WID]), ALU.mult), ("qb", b))
                do(v.tensor_reduce(sSc[:, :, b, :], kprod[:, :, :].rearrange("p g (h d) -> p g h d", h=H),
                                   AX.X, ALU.add), k_used)
            bk = arrived(v, ("sS",))
            do.release(v.tensor_copy(SS[:, 0:384], bk[0:64, 0:384]), ("sS",))
            v.wait_ge(ss_in, 16)
            do(ts(SS[:, 384:385], SS[:, 384:385], math.log(3.0), None, ALU.add))
            do(v.tensor_reduce(st[0:64, 140:141], SS[:, :], AX.X, ALU.max))
            do(ts(st[0:64, 141:142], st[0:64, 140:141], -1.0, None, ALU.mult), s_neg)
            v.wait_ge(s_exp, 1)
            do(v.reciprocal(st[0:64, 143:144], st[0:64, 142:143]))
            do(ts(SS[:, :], SS[:, :], st[0:64, 143:144], None, ALU.mult))
            do(ts(dP[:, :], ident[0:64, 0:64], SS[:, 384:385], None, ALU.mult), s_prob)
            bk = arrived(v, ("sP",))
            do(v.tensor_copy(PTs[:, :], bk[:, 0:192]))
            do.release(v.tensor_copy(Pd[:, :], bk[0:DB, 192:256]), ("sP",))
            v.wait_ge(v_used, DB)
            for c in range(4):
                for half in range(2):
                    ps = slice(64 * half, 64 * half + 64)
                    do(v.tensor_copy(mixT[ps, c, SEQ:NT], acc[0][ps, c * 64 + 2 * c + half:c * 64 + 64:8]), s_mixed)

            v.wait_ge(sml_in, SML_IN)
            v.wait_ge(c_in, 16)
            q_, k_, v_ = sml[:, 0:64], sml[:, 64:128], sml[:, 128:160]
            col = lambda n: sml[:, n:n + 1]
            n0 = par[:, P_N0:P_N0 + DH]
            do(tt(col(162), col(161), par[:, P_M0:P_M0 + 1], ALU.add))
            do(tt(col(320), col(162), col(160), ALU.max))
            do(tt(col(163), col(162), col(320), ALU.subtract))
            do(tt(col(164), col(160), col(320), ALU.subtract))
            do(ts(col(165), col(320), -1.0, None, ALU.mult), ms_ready)
            scale, gain, floor = col(166), col(167), col(168)
            bc_k = lambda x: x.unsqueeze(1).to_broadcast([P, 32, DH])
            do(v.tensor_tensor_reduce(sml[:, 330:394], q_, k_, 1.0, 0.0, ALU.mult, ALU.add, col(234)))
            do(v.tensor_tensor_reduce(sml[:, 330:394], q_, n0, 1.0, 0.0, ALU.mult, ALU.add, col(235)))
            do(tt(Ct[:, :, :], Cs[:, :, :], bc_k(q_), ALU.mult))
            do(v.tensor_reduce(sml[:, 202:234], Ct[:, :, :], AX.X, ALU.add))
            v.wait_ge(ms_exp, 1)
            do(tt(col(236), col(234), gain, ALU.mult))
            do(ts(sml[:, 202:234], sml[:, 202:234], scale, None, ALU.mult))
            do(stt(sml[:, 170:202], v_, col(236), sml[:, 202:234], ALU.mult, ALU.add))
            do(ts(col(237), col(235), scale, col(236), ALU.mult, ALU.add))
            do(stt(col(237), col(237), -1.0, col(237), ALU.mult, ALU.max))
            do(tt(col(237), col(237), floor, ALU.max))
            do(v.reciprocal(col(237), col(237)))
            do(ts(sml[:, 170:202], sml[:, 170:202], col(237), None, ALU.mult), ms_h)
            do(ts(sml[:, 256:320], n0, scale, None, ALU.mult))
            do(stt(sml[:, 256:320], k_, gain, sml[:, 256:320], ALU.mult, ALU.add))
            do(ts(Cs[:, :, :], Cs[:, :, :], scale, None, ALU.mult))
            do(tt(Ct[:, :, :], v_.unsqueeze(2).to_broadcast([P, 32, DH]), bc_k(k_), ALU.mult))
            do(stt(Cs[:, :, :], Ct[:, :, :], gain, Cs[:, :, :], ALU.mult, ALU.add), ms_C)

            for i in range(NTT):
                if i == NPT:
                    v.wait_ge(h4_in, 16)
                head_stat(hraw[0:rows(i), i, :], ht, i)
            inv_rms(DH)
            for i in range(NTT):
                r = rows(i)
                hr = hraw[0:r, i, :]
                h3 = hr.rearrange("p (h d) -> p h d", h=H)
                ss = ny[0:r, i * H:(i + 1) * H]
                do(tt(h3, h3, ss.unsqueeze(2).to_broadcast([r, H, DH]), ALU.mult))
                do(tt(hr, hr, par[0:r, P_GM:P_GM + WID], ALU.mult))
                emptied(v, ("mo", i))
                do(tt(hr, hr, sgo[0:r, i, :], ALU.mult), ml_norm)

            v.wait_ge(ms_out, MS_OUT)
            for m in range(KT):
                for f in range(2):
                    t = slice(f * HALF, (f + 1) * HALF)
                    bk = arrived(v, ("wo", m, f))
                    do.release(tt(xT[:, m, t], xT[:, m, t], bk[:, 0:HALF], ALU.add), ("wo", m, f))
                if m == 0:
                    arrived(v, ("mM", NTT - 1))
                do(tt(sqT[:, m, :], xT[:, m, :], xT[:, m, :], ALU.mult), sq2_done)
            for f in range(2):
                bk = arrived(v, ("n2", f))
                do.release(ts(msq[:, f * HALF:(f + 1) * HALF], bk[:, 0:HALF], 1.0 / D, EPS, ALU.mult, ALU.add),
                           ("n2", f))
            inv_sqrt(rstd2[:, :], msq[:, :], mtmp[:, :])
            for k in range(KT):
                do(stt(hT[:, k, :], xT[:, k, :], par[:, P_G2 + k:P_G2 + k + 1], rstd2[:, :], ALU.mult, ALU.mult),
                   h2_done)
            v.wait_ge(m_out, 16)
            v.wait_ge(scr_g, 32)
            for k in range(KT):
                do(v.tensor_copy(h_hi[:, k, :], hT[:, k, :]))
                do(tt(h_lo[:, k, :], hT[:, k, :], h_hi[:, k, :], ALU.subtract), hs_done)

            v.wait_ge(Cp_out, CP_OUT)

            def top16(val, ind, src):
                do(v.max(val[:, 0:8], src))
                do(v.max_index(ind[:, 0:8], val[:, 0:8], src))
                n = src.shape[1]
                do(v.match_replace(Srep[0:src.shape[0], 0:n], val[:, 0:8], src, LOWEST))
                do(v.max(val[:, 8:16], Srep[0:src.shape[0], 0:n]))
                do(v.max_index(ind[:, 8:16], val[:, 8:16], Srep[0:src.shape[0], 0:n]))

            for h in range(H):
                for i in range(NTT):
                    r = rows(i)
                    hk = slice(h * TOPK, (h + 1) * TOPK)
                    bk = arrived(v, ("sc", h, i))
                    do(v.tensor_copy(nv[0:r, i * H + h:i * H + h + 1], bk[0:r, 256:257]))
                    do.release(v.tensor_copy(Ssb[0:r, :, :], bk[0:r, 0:256].rearrange("p (a n) -> p a n", a=2)),
                               ("sc", h, i))
                    for a in range(2):
                        top16(vals[0:r, a, :], ixs[0:r, a, :], Ssb[0:r, a, :])
                    do(v.tensor_copy(I1[0:r, i, hk], ixs[0:r, 0, :]))
                    do(v.tensor_copy(I2[0:r, i, hk], ixs[0:r, 1, :]))
                    do(tt(cand[0:r, :, :], vals[0:r, 0, :].unsqueeze(2).to_broadcast([r, TOPK, TOPK]),
                          vals[0:r, 1, :].unsqueeze(1).to_broadcast([r, TOPK, TOPK]), ALU.add))
                    top16(SC[0:r, i, hk], CI[0:r, i, hk], cand[0:r, :, :].rearrange("p a b -> p (a b)"))

            inv_rms(2 * P)
            for i in range(NTT):
                r = rows(i)
                sc3 = SC[0:r, i, :].rearrange("p (h k) -> p h k", h=H)
                g3 = gt[0:r, :].rearrange("p (h k) -> p h k", h=H)
                if i >= 1:
                    arrived(v, ("tb", i - 1))
                do(tt(g3, sc3, sc3[:, :, 0:1].to_broadcast([r, H, TOPK]), ALU.subtract))
                do(tt(g3, g3, ny[0:r, i * H:(i + 1) * H].unsqueeze(2).to_broadcast([r, H, TOPK]), ALU.mult), g_sub)
                do(ts(abu[0:r, 0, :], CI[0:r, i, :], 4, None, ALU.logical_shift_right))
                do(ts(abu[0:r, 1, :], CI[0:r, i, :], 15, None, ALU.bitwise_and))
                do(v.tensor_copy(abf[0:r, :, :], abu[0:r, :, :]))
                for a, src in ((0, I1), (1, I2)):
                    do(tt(eq[0:r, :, :], abf[0:r, a, :].unsqueeze(2).to_broadcast([r, P, TOPK]),
                          iota[0:r, 0:TOPK].unsqueeze(1).to_broadcast([r, P, TOPK]), ALU.is_equal))
                    do(tt(eq[0:r, :, :].rearrange("p (h k) a -> p h k a", h=H),
                          eq[0:r, :, :].rearrange("p (h k) a -> p h k a", h=H),
                          src[0:r, i, :].rearrange("p (h a) -> p h a", h=H).unsqueeze(2).to_broadcast([r, H, TOPK, TOPK]),
                          ALU.mult))
                    do(v.tensor_reduce(idx[0:r, a, :], eq[0:r, :, :], AX.X, ALU.add))
                v.wait_ge(g_exp, i + 1)
                do(v.tensor_reduce(st[0:r, 150:158], g3, AX.X, ALU.add))
                do(v.reciprocal(st[0:r, 158:166], st[0:r, 150:158]))
                do(tt(g3, g3, st[0:r, 158:166].unsqueeze(2).to_broadcast([r, H, TOPK]), ALU.mult), tb_done)
                bk = arrived(v, ("tb", i))
                t = slice(i * P, i * P + r)
                do(v.tensor_copy(tables[:, 0, t], bk[:, 0:r]))
                do(v.tensor_copy(tables[:, 1, t], bk[:, P:P + r]))
                do(v.tensor_copy(ghb[:, 0:r], bk[:, 2 * P:2 * P + r]))
                do(v.tensor_copy(tables[:, 2, t], ghb[:, 0:r]))
                do.release(tt(tables[:, 3, t], bk[:, 2 * P:2 * P + r], tables[:, 2, t], ALU.subtract), ("tb", i))

            def gate_rows(n, b, i):
                wait_pos(v, gl_R, (n - 1) * QUADS)
                wait_pos(v, gl_L, (n - 1) * QUADS)
                v.tensor_copy(cur[b][:, :, :], tables[:, :, bass.ds(n * TB, TB)]).then_inc(cur_done, 1)
                v.wait_ge(cur_done, n + 1)
                for q in range(QUADS):
                    slot = q % 5
                    wait_pos(v, gl_mm, n * QUADS + (q - 4))
                    for t in range(4):
                        k = 4 * q + t
                        for part in range(2):
                            ins = ts(gateL[slot][:, t, part, :], iota_b[:, :], cur[b][:, 0, k:k + 1],
                                     cur[b][:, 2 + part, k:k + 1], ALU.is_equal, ALU.mult)
                    ins.then_inc(gl_L, 1)

            blocks(v, gate_rows)

            def u_low(g, s):
                v.wait_ge(uhi_done, g.n * 4 + s + 1)
                tt(u_lo[g.b][:, 2 * s:2 * s + 2, :], u_raw[g.b][:, 2 * s:2 * s + 2, :],
                   u_hi[g.b][:, 2 * s:2 * s + 2, :], ALU.subtract).then_inc(ulo_done, 1)

            def v_low(g, s):
                v.wait_ge(vhi_done, g.n * 4 + s + 1)
                tt(v_lo[g.b][:, s, :], v_raw[g.b][:, s, :], v_hi[g.b][:, s, :], ALU.subtract).then_inc(vlo_done, 1)

            def gated(g):
                v.wait_ge(gg_in[g.b], (g.i + 1) * 16)
                wait_pos(v, b_made, (g.n - 1) * KT)
                for c in range(GC):
                    u = g.n * GC + c
                    v.wait_ge(a_gelu, u + 1)
                    wf = w_f[c % 2]
                    tt(wf[:, :].rearrange("p (a t) -> p a t", a=NBLK),
                       act_f[c % 2][:, :].rearrange("p (a t) -> p a t", a=NBLK), g_in[g.b][:, :, c, :],
                       ALU.mult).then_inc(w_prod, 1)
                    v.wait_ge(w_prod, u + 1)
                    v.tensor_copy(w_hi[g.b][:, c, :], wf[:, :]).then_inc(whi_done, 1)
                    v.wait_ge(whi_done, u + 1)
                    tt(w_lo[g.b][:, c, :], wf[:, :], w_hi[g.b][:, c, :], ALU.subtract).then_inc(wlo_done, 1)

            def dve_step(g, last):
                more = not (last and g.b == 1)
                if more:
                    gated(g.plus(1))
                for m in range(KT):
                    v.wait_ge(b_made, g.n * KT + m + 1)
                    x3 = xT[:, m, :].rearrange("p (f t) -> p f t", f=2)
                    tt(x3, x3, bbank[m % 2][:, :, 0:HALF], ALU.add).then_inc(b_added, 1)
                    if 1 <= m < 5 and not last:
                        u_low(g.plus(2), m - 1)
                    if m >= 4 and more:
                        v_low(g.plus(1), m - 4)

            v.wait_ge(gl_mm, NBLK * QUADS)
            first = Group(0, 0)
            for s in range(4):
                u_low(first, s)
            for s in range(4):
                u_low(first.plus(1), s)
            for s in range(4):
                v_low(first, s)
            gated(first)
            groups(v, dve_step)

        @blk.tensor
        def _(pe):
            def product(dst, pairs, key=None):
                for n, (l, r) in enumerate(pairs):
                    mm = pe.matmul(dst, l, r, start=(n == 0), stop=(n == len(pairs) - 1))
                if key:
                    made(mm, key)
                return mm

            def turn(dst, src, n):
                return pe.transpose(dst, src, ident[0:n, 0:n])

            halves = [slice(0, HALF), slice(HALF, NT)]
            pe.wait_ge(ones_set, 1)
            pe.wait_ge(const_in, 32)
            for f in range(2):
                bk = claim(pe, ("n1", f))
                if f == 0:
                    pe.wait_ge(sq_done, KT)
                product(bk[:, 0:HALF], [(ones[:, :], sqT[:, k, halves[f]]) for k in range(KT)], ("n1", f))
            pe.wait_ge(h_done, KT)
            pe.wait_ge(wg_in, 16)
            for n, g in enumerate(("gi", "gf")):
                for f in range(2):
                    bk = claim(pe, (g, f))
                    product(bk[0:H, 0:HALF], [(wg[:, k, n * H:(n + 1) * H], hT[:, k, halves[f]]) for k in range(KT)],
                            (g, f))
            for c in range(8):
                w = weights_arrived(pe, f"mqk{c // 4}")
                for f in range(2):
                    bk = claim(pe, ("mqk", c, f))
                    product(bk[:, 0:HALF], [(w[:, k, (c % 4) * P:(c % 4 + 1) * P], hT[:, k, halves[f]])
                                            for k in range(KT)], ("mqk", c, f))
            for g in ("q", "k", "v", "mv", "mo"):
                w = weights_arrived(pe, g)
                for i in range(NTT):
                    r = rows(i)
                    bk = claim(pe, (g, i))
                    product(bk[0:r, :], [(hT[:, k, i * P:i * P + r], w[:, k, :]) for k in range(KT)], (g, i))
            pe.wait_ge(rope_done, 2 * NTT)
            for i in range(NPT):
                for g, z in (("qT", zq), ("kT", zk)):
                    bk = claim(pe, (g, i))
                    for c in range(4):
                        mm = turn(bk[:, c * P:(c + 1) * P], z[:, i, c * P:(c + 1) * P], P)
                    made(mm, (g, i))
            for i in range(NPT):
                emptied(pe, ("qT", i))
                emptied(pe, ("kT", i))
                emptied(pe, ("v", i))

            def scores(i, h):
                bk = claim(pe, ("S", i, h))
                ps = slice(64 * (h % 2), 64 * (h % 2) + 64)
                product(bk[:, 0:(i + 1) * P], [(qT[ps, h // 2, i * P:(i + 1) * P], kT[ps, h // 2, 0:(i + 1) * P])],
                        ("S", i, h))

            scores(0, 0)
            for n, (i, h) in enumerate(ATT):
                if n + 1 < len(ATT):
                    scores(*ATT[n + 1])
                bk = claim(pe, ("PT", i, h))
                pe.wait_ge(att_exp, n + 1)
                for j in range(i + 1):
                    mm = turn(bk[:, j * P:(j + 1) * P], Pb[n % 2][:, j * P:(j + 1) * P], P)
                made(mm, ("PT", i, h))
                emptied(pe, ("PT", i, h))
                if h == 0 and i >= 2:
                    pe.wait_ge(att_out, i - 1)
                product(acc[i % 2][:, h * DH:(h + 1) * DH],
                        [(PTb[n % 2][:, j, :], zv[:, j, h * DH:(h + 1) * DH]) for j in range(i + 1)]
                        ).then_inc(att_pv, 1)
            pe.wait_ge(enm_done, 1)
            bk = claim(pe, ("aT",))
            for n, src in enumerate((arow, enm)):
                for i in range(NPT):
                    mm = turn(bk[:, n * 32 + i * H:n * 32 + (i + 1) * H], src[:, i * P:(i + 1) * P], H)
            made(mm, ("aT",))
            pe.wait_ge(kscaled, 4)
            for i in range(NPT):
                bk = claim(pe, ("kt", i))
                for c in range(4):
                    mm = turn(bk[:, c * P:(c + 1) * P], qkT[:, 4 + c, i * P:(i + 1) * P], P)
                made(mm, ("kt", i))
            for n, key in enumerate((("sq",), ("sk",))):
                bk = claim(pe, key)
                for c in range(4):
                    mm = turn(bk[0:DB, c * P:(c + 1) * P], qkT[:, 4 * n + c, SEQ:NT], P)
                made(mm, key)

            def minus_max(h):
                bk = claim(pe, ("nM", h))
                product(bk[:, :], [(sel[:, h, :], nrow[:, 0:SEQ])], ("nM", h))

            pe.wait_ge(sel_in, 16)
            minus_max(0)
            for h in range(H):
                b = h % 2
                if h + 1 < H:
                    minus_max(h + 1)
                ps = slice(64 * b, 64 * b + 64)
                for j in range(NPT):
                    w = (NPT - j) * P
                    bk = claim(pe, ("ST", h, j))
                    product(bk[:, 0:w], [(qkT[ps, 4 + h // 2, j * P:(j + 1) * P], qkT[ps, h // 2, j * P:SEQ])],
                            ("ST", h, j))
                bk = claim(pe, ("num", h))
                for j in range(NPT):
                    emptied(pe, ("ST", h, j))
                if h == 0:
                    for i in range(NPT):
                        emptied(pe, ("mv", i))
                for i in range(NPT):
                    mm = product(bk[:, i * (DH + 1):(i + 1) * (DH + 1)],
                                 [(sdm[b][:, OJ[j] + (i - j) * P:OJ[j] + (i - j + 1) * P], mv1[:, j, h, :])
                                  for j in range(i + 1)])
                made(mm, ("num", h))
                bk = claim(pe, ("C", h))
                pe.wait_ge(ml_wk, NPT * (h + 1))
                product(bk[0:DH + 1, 0:DH], [(mv1[:, j, h, :], wk[b][:, j, :]) for j in range(NPT)], ("C", h))

            for b in range(DB):
                bk = claim(pe, ("qb", b))
                product(bk[:, :], [(sel[:, b, :], zq[0:DB, NPT, :])], ("qb", b))
            bk = claim(pe, ("sS",))
            pe.wait_ge(k_used, DB)
            for g in range(3):
                mm = turn(bk[0:64, g * P:(g + 1) * P], sSc[:, g, :, :].rearrange("p b h -> p (b h)"), P)
            made(mm, ("sS",))
            bk = claim(pe, ("sP",))
            pe.wait_ge(s_prob, 1)
            for g in range(3):
                turn(bk[:, g * 64:(g + 1) * 64], SS[:, g * P:(g + 1) * P], 64)
            product(bk[0:DB, 192:256], [(seld, dP[:, :])], ("sP",))
            emptied(pe, ("sP",))
            pe.wait_ge(att_out, NPT)
            for c in range(4):
                pe.matmul(acc[0][:, c * 64:(c + 1) * 64], zv[0:DB, NPT, c * P:(c + 1) * P], Pd[:, :],
                          start=(c == 0), stop=False, skip_group_check=True)
            for b in range(DB):
                m = DB + b
                pe.wait_ge(kv_in[m % NKV], 48 * (m // NKV + 1))
                for g in range(3):
                    for c in range(4):
                        mm = pe.matmul(acc[0][:, c * 64 + b * H:c * 64 + (b + 1) * H],
                                       kv[m % NKV][:, g, c * P:(c + 1) * P], PTs[:, g * 64 + b * H:g * 64 + (b + 1) * H],
                                       start=False, stop=(g == 2), skip_group_check=True)
                mm.then_inc(v_used, 1)

            for i in range(NPT):
                bk = claim(pe, ("mA", i))
                for c in range(4):
                    mm = turn(bk[:, c * P:(c + 1) * P], atok[:, i, c * P:(c + 1) * P], P)
                made(mm, ("mA", i))
            for i in range(NTT):
                r = rows(i)
                bk = claim(pe, ("mM", i))
                pe.wait_ge(ml_norm, i + 1)
                for c in range(4):
                    mm = turn(bk[:, c * r:(c + 1) * r], hraw[0:r, i, c * P:(c + 1) * P], r)
                made(mm, ("mM", i))
            for i in range(NPT):
                emptied(pe, ("mA", i))
            for i in range(NTT):
                emptied(pe, ("mM", i))
            pe.wait_ge(s_mixed, 8)
            for m in range(KT):
                w = weights_arrived(pe, f"wo{m // 4}")
                for f in range(2):
                    bk = claim(pe, ("wo", m, f))
                    product(bk[:, 0:HALF], [(w[:, k, (m % 4) * P:(m % 4 + 1) * P], mixT[:, k, halves[f]])
                                            for k in range(KT)], ("wo", m, f))
            for f in range(2):
                bk = claim(pe, ("n2", f))
                pe.wait_ge(sq2_done, KT)
                product(bk[:, 0:HALF], [(ones[:, :], sqT[:, k, halves[f]]) for k in range(KT)], ("n2", f))
            pe.wait_ge(h2_done, KT)
            pe.wait_ge(sk_in, 16)

            def query(h):
                for m in (2 * h, 2 * h + 1):
                    w = weights_arrived(pe, f"wq{m // 4}")
                    for f in range(2):
                        bk = claim(pe, ("wq", m, f))
                        product(bk[:, 0:HALF], [(w[:, k, (m % 4) * P:(m % 4 + 1) * P], hT[:, k, halves[f]])
                                                for k in range(KT)], ("wq", m, f))

            query(0)
            for h in range(H):
                if h + 1 < H:
                    query(h + 1)
                for m in (2 * h, 2 * h + 1):
                    for f in range(2):
                        emptied(pe, ("wq", m, f))
                for i in range(NTT):
                    t = slice(i * P, i * P + rows(i))
                    bk = claim(pe, ("sc", h, i))
                    for a in range(2):
                        product(bk[0:rows(i), a * P:(a + 1) * P], [(qg[h % 2][:, a, t], skT[:, 2 * h + a, :])])
                    product(bk[0:rows(i), 256:257], [(qsq[h % 2][:, a, t], ones[:, 0:1]) for a in range(2)],
                            ("sc", h, i))
            for i in range(NTT):
                r = rows(i)
                bk = claim(pe, ("tb", i))
                pe.wait_ge(tb_done, i + 1)
                for n, src in enumerate((idx[0:r, 0, :], idx[0:r, 1, :], gt[0:r, :])):
                    mm = turn(bk[:, n * P:n * P + r], src, r)
                made(mm, ("tb", i))
            for i in range(NTT):
                emptied(pe, ("tb", i))

            def gates(n, b, i):
                for q in range(QUADS):
                    u = n * QUADS + q
                    pe.wait_ge(gl_L, u + 1)
                    pe.wait_ge(gl_R, u + 1)
                    wait_pos(pe, gl_ev, u - 4)
                    for t in range(4):
                        for part in range(2):
                            mm = pe.matmul(gbank[q % 5][:, t * P:(t + 1) * P], oneR[q % 5][:, t, :],
                                           gateL[q % 5][:, t, part, :], start=(part == 0), stop=(part == 1))
                    mm.then_inc(gl_mm, 1)

            blocks(pe, gates)

            def up(g):
                b = g.b
                pe.wait_ge(ulo_done, g.n * 4 + 4)
                for c in range(GC):
                    wait_pos(pe, a_gelu, g.n * GC + c - 1)
                    for k in range(KT):
                        for n, (w, hs) in enumerate(((u_hi, h_hi), (u_hi, h_lo), (u_lo, h_hi))):
                            for f in range(2):
                                mm = pe.matmul(abank[c % 2][:, f, 0:HALF], w[b][:, k, c * P:(c + 1) * P],
                                               hs[:, k, halves[f]], start=(k == 0 and n == 0),
                                               stop=(k == KT - 1 and n == 2))
                    mm.then_inc(a_made, 1)

            def down(g):
                b = g.b
                pe.wait_ge(vlo_done, g.n * 4 + 4)
                pe.wait_ge(wlo_done, g.n * GC + GC)
                for m in range(KT):
                    wait_pos(pe, b_added, g.n * KT + m - 1)
                    for c in range(GC):
                        for n, (w, x) in enumerate(((v_hi, w_hi), (v_hi, w_lo), (v_lo, w_hi))):
                            for f in range(2):
                                mm = pe.matmul(bbank[m % 2][:, f, 0:HALF], w[b][:, c, m * P:(m + 1) * P],
                                               x[b][:, c, halves[f]], start=(c == 0 and n == 0),
                                               stop=(c == GC - 1 and n == 2))
                    mm.then_inc(b_made, 1)

            def pe_step(g, last):
                if not (last and g.b == 1):
                    up(g.plus(1))
                down(g)

            pe.wait_ge(gl_ev, NBLK * QUADS)
            up(Group(0, 0))
            groups(pe, pe_step)


def constants():
    import numpy as np

    c = np.zeros((P, C_END), np.float32)
    c[:, C_IDENT:C_IDENT + P] = np.eye(P)
    c[:, C_IOTA:C_IOTA + P] = np.arange(P)
    p = np.arange(P)[:, None]
    dist = 384 + p - np.arange(SEQ)[None, :]
    count = sum(((dist >= 0) & (dist <= w) & (dist % d == 0)).astype(np.int64) for w, d in DIL)
    c[:, C_MASK:C_MASK + SEQ] = np.where(count > 0, np.log(np.maximum(count, 1)), NEG)
    c[:, C_CAUSAL:C_CAUSAL + P] = np.where(np.arange(P)[None, :] >= p, 0.0, NEG)
    inv = (10000.0 ** (-np.arange(32) / 32.0)).astype(np.float32)
    pos = np.full(P * NTT, 4096, np.float32)
    pos[:SEQ] = np.arange(SEQ)
    ang = (pos[:, None] * inv[None, :]).astype(np.float32)
    for at, fn in ((C_COS, np.cos), (C_SIN, np.sin)):
        t = fn(ang.astype(np.float64)).astype(np.float32).reshape(NTT, P, 32)
        c[:, at:at + 160] = t.transpose(1, 0, 2).reshape(P, 160)
    c[0:64, C_SEL:C_END] = (np.arange(64)[:, None] // H == np.arange(DB)[None, :])
    sel = np.zeros((H, H, P), np.float32)
    for h in range(H):
        sel[h, h, :] = 1.0
    return c, sel


def kernel(x_prompt, x_sample, cache_attn_k, cache_attn_v, state_mlstm_C, state_mlstm_n, state_mlstm_m,
           state_mlstm_conv, norm1_g, w_in, att_qnorm_g, att_knorm_g, b_gates, mlstm_conv_w, mlstm_conv_b,
           mlstm_norm_g, w_out, norm2_g, peer_w_query, peer_qnorm_g, peer_subkeys, peer_u, peer_v):
    import numpy as np
    import concourse.bacc as bacc
    from concourse import mybir as mb
    from concourse.bass_utils import run_bass_kernel_spmd as run

    A = np.ascontiguousarray

    def by_part(w):
        w = np.asarray(w)
        return w.reshape(-1, P, w.shape[-1]).transpose(1, 0, 2)

    x_all = np.concatenate([np.asarray(x_prompt).reshape(SEQ, D), np.asarray(x_sample).reshape(DB, D)])
    w = np.asarray(w_in)[0]
    at = dict(q=0, k=WID, v=2 * WID, mqk0=3 * WID, mqk1=4 * WID, mv=5 * WID, mo=6 * WID + 16)
    wo, wq = np.asarray(w_out)[0], np.asarray(peer_w_query)[0]
    groups = []
    for g in WGROUPS:
        if g in at:
            groups.append(w[:, at[g]:at[g] + 512])
        else:
            src = wo if g[:2] == "wo" else wq
            n = int(g[2:])
            groups.append(src[:, n * 512:(n + 1) * 512])
    const, sel = constants()
    par = np.zeros((P, P_END), np.float32)
    par[:, P_G1:P_G1 + 8] = np.asarray(norm1_g)[0].reshape(KT, P).T
    par[:, P_G2:P_G2 + 8] = np.asarray(norm2_g)[0].reshape(KT, P).T
    par[:, P_GQN:P_GQN + 2] = np.asarray(peer_qnorm_g)[0].reshape(2, P).T
    par[:, P_CW:P_CW + 32] = np.asarray(mlstm_conv_w)[0].reshape(CW, KT, P).transpose(2, 1, 0).reshape(P, 32)
    par[:, P_CB:P_CB + 8] = np.asarray(mlstm_conv_b)[0].reshape(KT, P).T
    par[:, P_GQ:P_GQ + DH] = np.asarray(att_qnorm_g)[0]
    par[:, P_GK:P_GK + DH] = np.asarray(att_knorm_g)[0]
    par[:, P_GM:P_GM + WID] = np.asarray(mlstm_norm_g)[0]
    par[0:H, P_BG8:P_BG8 + 2] = np.asarray(b_gates)[0].reshape(2, H).T
    par[:, P_M0] = np.repeat(np.asarray(state_mlstm_m)[0].reshape(-1), 2)
    par[:, P_N0:P_N0 + DH] = np.repeat(np.asarray(state_mlstm_n)[0].reshape(-1, DH), 2, axis=0)
    ins = dict(
        const=const, par=par, sel=sel,
        xT=A(by_part(x_all.T)),
        wg=A(by_part(w[:, 6 * WID:6 * WID + 16])),
        w=A(np.stack([by_part(g) for g in groups])),
        cst=A(np.asarray(state_mlstm_conv)[0].reshape(DB, 3, KT, P).transpose(3, 2, 1, 0)),
        ck=A(np.asarray(cache_attn_k)[0].reshape(DB, NCACHE, WID)),
        cv=A(np.asarray(cache_attn_v)[0].reshape(DB, NCACHE, WID)),
        C0=A(np.asarray(state_mlstm_C)[0].reshape(P, 32, DH)),
        sk=A(np.asarray(peer_subkeys)[0].reshape(2 * H, NKEYS, P).transpose(2, 0, 1)),
        uT=A(np.asarray(peer_u)[0].reshape(NG, GC * P, KT, P).transpose(0, 3, 2, 1).reshape(NG, P, KT * GC * P)),
        v=A(np.asarray(peer_v)[0].reshape(NG, GC, P, D).transpose(0, 2, 1, 3).reshape(NG, P, GC * D)),
    )
    outs = dict(
        yT=(P, KT, NT), kp=(NPT, P, WID), vp=(NPT, P, WID), ks=(DB, WID), vs=(DB, WID),
        Cp=(H, DH, DH), np=(1, H, DH), mp=(H, 1), convp=(P, KT, 3), convs=(P, KT, 3, DB),
        Cs=(P, 32, DH), ns=(DB * H, DH), ms=(DB * H, 1),
    )
    nc = bacc.Bacc("TRN2", target_bir_lowering=False, num_devices=1)
    arrays = {f"in_{n}": a for n, a in ins.items()}
    I = {n: nc.dram_tensor(f"in_{n}", a.shape, mb.dt.from_np(a.dtype), kind="ExternalInput").ap() for n, a in ins.items()}
    O = {n: nc.dram_tensor(f"out_{n}", s, F32, kind="ExternalOutput").ap() for n, s in outs.items()}
    trunk_and_peer(nc, I, O)
    r = run(nc, [arrays], core_ids=[0]).results[0]
    o = {n: r[f"out_{n}"] for n in outs}
    y = o["yT"].transpose(2, 1, 0).reshape(NT, D)
    return (
        A(y[:SEQ]).reshape(1, SEQ, D), A(y[SEQ:]).reshape(DB, 1, D),
        o["kp"].reshape(1, 1, SEQ, H, DH), o["vp"].reshape(1, 1, SEQ, H, DH),
        o["ks"].reshape(1, DB, 1, H, DH), o["vs"].reshape(1, DB, 1, H, DH),
        o["Cp"].reshape(1, 1, H, DH, DH), o["np"].reshape(1, 1, H, DH), o["mp"].reshape(1, 1, H),
        A(o["convp"].transpose(2, 1, 0)).reshape(1, 1, 3, D),
        o["Cs"].reshape(1, DB, H, DH, DH), o["ns"].reshape(1, DB, H, DH), o["ms"].reshape(1, DB, H),
        A(o["convs"].transpose(3, 2, 1, 0)).reshape(1, DB, 3, D),
    )
```

```python
import math

import concourse.bass as bass
from concourse import mybir

F32 = mybir.dt.float32
BF16 = mybir.dt.bfloat16
U32 = mybir.dt.uint32
ALU = mybir.AluOpType
ACT = mybir.ActivationFunctionType
AX = mybir.AxisListType

P = 128
D = 1024
KT = D // P
SEQ = 512
DB = 8
NT = SEQ + DB
HALF = NT // 2
NPT = SEQ // P
NTT = NPT + 1
H = 8
DH = 64
WID = H * DH
CW = 4
TOPK = 16
NKEYS = 128
EPS = 1e-6
NEG = -1e30
LOWEST = -3.0e38
NCACHE = 2048
DIL = ((128, 1), (512, 4), (2048, 16))
GC = 4
NG = NKEYS // GC
TB = 40
NBLK = NT // TB
QUADS = TB // 4
PAIRS = QUADS // 2
NKV = 2
RING = 6

C_IDENT, C_IOTA, C_MASK, C_CAUSAL, C_COS, C_SIN, C_SEL, C_SELH, C_END = 0, 128, 256, 768, 896, 1056, 1216, 1224, 1232
P_G1, P_G2, P_GQN, P_CW, P_CB, P_GQ, P_GK, P_GM, P_BG8, P_M0, P_N0, P_END = (
    0, 8, 16, 18, 50, 58, 122, 186, 698, 700, 701, 768)

WGROUPS = ["mqk0", "mqk1", "q", "k", "v", "mv", "mo", "wo0", "wo1", "wq0", "wq1", "wq2", "wq3"]


def rows(i):
    return P if i < NPT else DB


def queries_before(h):
    return [0] if h == 0 else [1, 2] if h == 1 else [h + 1] if h + 1 < H else []


def psum_plan():
    u = [("n1", f) for f in range(2)]
    u += [(g, f) for g in ("gi", "gf") for f in range(2)]
    u += [("mqk", c, f) for c in range(8) for f in range(2)]
    u += [(g, i) for g in ("q", "k", "v") for i in range(NTT)]
    u += [("mv", NPT), ("sq",), ("sk",)]
    for i in range(NPT):
        u += [("mv", i)] + [("qb", b) for b in (2 * i, 2 * i + 1)]
    u += [("mo", 0), ("sS",), ("mo", 1), ("sP",)] + [("mo", i) for i in range(2, NTT)]
    u += [(g, i) for i in range(NPT) for g in ("qT", "kT")]
    att = [(i, h) for i in range(NPT) for h in range(H)]
    u += [("S", *att[0]), ("S", *att[1])]
    for n, (i, h) in enumerate(att):
        if n + 2 < len(att):
            u += [("S", *att[n + 2])]
        u += [("PT", i, h)]
    u += [("aT",)] + [("kt", i) for i in range(NPT)]
    u += [("nM", 0)]
    for h in range(H):
        if h + 1 < H:
            u += [("nM", h + 1)]
        u += [("ST", h, j) for j in range(NPT)] + [("num", h), ("C", h)]
    u += [("mA", i) for i in range(NPT)] + [("mM", i) for i in range(NTT)]
    u += [("wo", m, f) for m in range(8) for f in range(2)]
    u += [("n2", f) for f in range(2)]
    for h in range(H):
        u += [("wq", m, f) for g in queries_before(h) for m in (2 * g, 2 * g + 1) for f in range(2)]
        u += [("sc", h, i) for i in range(NPT)]
    u += [("sc", H, NPT)] + [("tb", i) for i in range(NTT)]
    return {key: n for n, key in enumerate(u)}


def trunk_and_peer(nc, I, O):
    sem = nc.alloc_semaphore
    place = psum_plan()
    full = [sem(f"psum_full{k}") for k in range(RING)]
    free = [sem(f"psum_free{k}") for k in range(RING)]
    pa = nc.alloc_psum_tensor("psum", [P, 8, 512], F32)
    bank = [pa[:, k, :] for k in range(RING)]
    acc = [pa[:, RING + k, :] for k in range(2)]

    def bank_of(key):
        return bank[place[key] % RING]

    def claim(eng, key):
        n = place[key]
        if n >= RING:
            eng.wait_ge(free[n % RING], n // RING)
        return bank[n % RING]

    def made(ins, key):
        ins.then_inc(full[place[key] % RING], 1)

    def arrived(eng, key):
        n = place[key]
        eng.wait_ge(full[n % RING], n // RING + 1)
        return bank[n % RING]

    def release(ins, key):
        ins.then_inc(free[place[key] % RING], 1)

    def emptied(eng, key):
        n = place[key]
        eng.wait_ge(free[n % RING], n // RING + 1)

    base = (nc.sbuf_base + 63) // 64 * 64

    def put(name, shape, dt, off):
        return nc.alloc_sbuf_tensor_at(name, shape, dt, offset=off)

    HT = KT * NT * 4
    a0 = base
    xT = put("xT", [P, KT, NT], F32, a0)
    hs0 = a0 + HT
    h_hi = put("h_hi", [P, KT, NT], BF16, hs0)
    h_lo = put("h_lo", [P, KT, NT], BF16, hs0 + HT // 2)
    ig, fx, lf, ax, lfm, cumB, nrow, mrow = [put(n, [H, NT], F32, hs0 + 2080 * k) for k, n in enumerate(
        ["ig", "fx", "lf", "ax", "lfm", "cumB", "nrow", "mrow"])]
    c0 = hs0 + HT
    tables = put("tables", [P, 4, NT], BF16, c0)
    ones_row = put("ones_row", [H, SEQ], F32, c0)
    arow = put("arow", [H, SEQ], F32, c0 + 2048)
    enm = put("enm", [H, SEQ], F32, c0 + 4096)
    sSc = put("sSc", [P, 3, DB, H], F32, c0 + 6144)
    PTs = put("PTs", [P, 192], F32, c0 + 6912)
    dP = put("dP", [64, 64], F32, c0 + 7680)
    Pd = put("Pd", [DB, 64], F32, c0 + 7936)
    k0 = c0 + 4 * NT * 4
    const = put("const", [P, C_END], F32, k0)
    par = put("par", [P, P_END], F32, k0 + C_END * 4)
    sel = put("sel", [H, H, P], F32, k0 + (C_END + P_END) * 4)
    ones = put("ones", [P, P], F32, k0 + (C_END + P_END + 1024) * 4)
    st = put("stats", [P, 384], F32, k0 + (C_END + P_END + 1024 + 128) * 4)
    e0 = k0 + (C_END + P_END + 1024 + 128 + 384) * 4
    decT = st[:, 320:320 + 4 * DB].rearrange("p (c b) -> p c b", c=4)
    nv, na, ny = st[:, 192:232], st[:, 232:272], st[:, 272:312]
    ident = const[:, C_IDENT:C_IDENT + P]
    iota = const[:, C_IOTA:C_IOTA + P]
    maskt = const[:, C_MASK:C_MASK + SEQ]
    causal = const[:, C_CAUSAL:C_CAUSAL + P]
    cosT = const[:, C_COS:C_SIN].rearrange("p (i r) -> p i r", r=32)
    sinT = const[:, C_SIN:C_SEL].rearrange("p (i r) -> p i r", r=32)
    seld = const[0:64, C_SEL:C_SELH]
    selh = const[0:64, C_SELH:C_END]

    B0 = e0
    hT = put("hT", [P, KT, NT], F32, B0)
    qT = put("qT", [P, 4, SEQ], F32, B0)
    kT = put("kT", [P, 4, SEQ], F32, B0 + 8192)
    C0 = B0 + HT
    sqT = put("sqT", [P, KT, NT], F32, C0)
    mqkT = put("mqkT", [P, KT, NT], F32, C0)
    hraw = put("hraw", [P, NTT, WID], F32, C0)
    dm = put("dm", [P, NPT, P], F32, C0 + 10240)
    ht = put("ht", [P, WID], F32, C0 + 12288)
    SS = put("SS", [64, 385], F32, C0 + 14336)
    qg = [put(f"qg{b}", [P, 2, NT], F32, C0 + 4160 * b) for b in range(2)]
    qsq = [put(f"qsq{b}", [P, 2, NT], F32, C0 + 8320 + 4160 * b) for b in range(2)]
    kv = [put(f"kv{b}", [P, 3, WID], F32, C0 + 6144 * b) for b in range(NKV)]
    qks = [put("qks0", [DB, WID], F32, C0 + 12288)]
    D0 = C0 + HT
    qkT = put("qkT", [P, KT, NT], F32, D0)
    mixT = put("mixT", [P, KT, NT], F32, D0)
    E0 = D0 + HT
    zq = put("zq", [P, NTT, WID], F32, E0)
    zk = put("zk", [P, NTT, WID], F32, E0 + 10240)
    atok = put("atok", [P, NPT, WID], F32, E0)
    ktok = put("ktok", [P, NPT, WID], F32, E0 + 10240)
    F0 = E0 + 20480
    zv = put("zv", [P, NTT, WID], F32, F0)
    Cst = put("Cst", [DH + 1, H, DH], F32, F0 + 4096)
    sgo = put("sgo", [P, NTT, WID], F32, F0 + 10240)
    skT = put("skT", [P, 2 * H, P], F32, F0 + 10240)
    mv1 = put("mv1", [P, NTT, H, DH + 1], F32, F0 + 20480)
    G0 = F0 + 20480 + 10400
    Sb = [put(f"Sb{b}", [P, SEQ], F32, G0 + 2048 * b) for b in range(3)]
    Pb = [put(f"Pb{b}", [P, SEQ], F32, G0 + 6144 + 2048 * b) for b in range(3)]
    PTb = [put(f"PTb{b}", [P, NPT, P], F32, G0 + 12288 + 2048 * b) for b in range(3)]
    rt = put("rt", [P, WID], F32, G0 + 12288)
    rt2 = put("rt2", [P, WID], F32, G0 + 14336)
    rstd = put("rstd", [P, NT], F32, G0 + 16384)
    msq, mtmp = [put(n, [P, NT], F32, G0 + 8192 + 2080 * k) for k, n in enumerate(["msq", "mtmp"])]
    OJ = [0, 512, 896, 1152]
    Dm = [put(f"Dm{b}", [P, 1280], F32, G0 + 5120 * b) for b in range(2)]
    sdm = [put(f"sdm{b}", [P, 1280], F32, G0 + 10240 + 5120 * b) for b in range(2)]
    Cs = put("Cs", [P, 32, DH], F32, G0)
    Ct = put("Ct", [P, 32, DH], F32, G0 + 8192)
    kprod = put("kprod", [P, 3, WID], F32, G0 + 8192)
    sml = put("sml", [P, 512], F32, G0 + 16384)
    rstd2 = put("rstd2", [P, NT], F32, G0)
    W0 = G0 + 20480
    qks.append(put("qks1", [DB, WID], F32, W0 + 32768))
    wr = [put(f"wr{b}", [P, KT, 512], F32, W0 + 16384 * b) for b in range(2)]
    X0 = W0 + 32768
    wg = put("wg", [P, KT, 16], F32, X0)
    cst = put("cst", [P, KT, 3, DB], F32, X0 + 512)
    convt = put("convt", [P, KT, 3, DB], F32, X0 + 1280)
    wk = [put(f"wk{b}", [P, NPT, DH], F32, X0 + 1024 * b) for b in range(2)]
    assert X0 + 2048 <= nc.sbuf_usable_end, (X0 + 2048 - nc.sbuf_usable_end)
    vals = [put(f"vals{b}", [P, 2, TOPK], F32, E0 + 128 * b) for b in range(2)]
    ixs = [put(f"ixs{b}", [P, 2, TOPK], U32, E0 + 256 + 128 * b) for b in range(4)]
    CI = [put(f"CI{b}", [P, TOPK], U32, E0 + 768 + 64 * b) for b in range(2)]
    abu = put("abu", [P, 2, TOPK], U32, E0 + 896)
    abf = put("abf", [P, 2, TOPK], BF16, E0 + 1024)
    ranks16 = put("ranks16", [P, TOPK, TOPK], BF16, E0 + 1088)
    Ssb = [put(f"Ssb{b}", [P, 2, P], F32, E0 + 1600 + 1024 * b) for b in range(3)]
    rest = put("rest", [P, 2, P], F32, E0 + 4672)
    crest = put("crest", [P, TOPK * TOPK], F32, E0 + 5696)
    cand = put("cand", [P, TOPK, TOPK], F32, E0 + 6720)
    SC = put("SC", [P, NTT, P], F32, E0 + 7744)
    gt = put("gt", [P, NTT, P], F32, E0 + 10304)
    idx = put("idx", [P, NTT, 2, P], F32, E0 + 12864)
    M0 = F0 + 20480
    eq = [put(f"eq{b}", [P, 2, TOPK, TOPK], BF16, M0 + 1024 * b) for b in range(2)]
    ixf = put("ixf", [P, 2, TOPK], F32, M0 + 2048)
    picked = put("picked", [P, 2, TOPK, TOPK], F32, M0 + 2176)
    fold8 = put("fold8", [P, 2, 8, TOPK], F32, M0 + 4224)
    fold4 = put("fold4", [P, 2, 4, TOPK], F32, M0 + 5248)
    fold2 = put("fold2", [P, 2, 2, TOPK], F32, M0 + 5760)
    byrow = put("byrow", [64, 3, P], F32, M0 + 6016)
    qz = put("qz", [P, 2, H, 64], F32, D0)
    qzsq = put("qzsq", [P, 2, H, 64], F32, D0 + 4096)

    L0 = c0 + 4 * NT * 2
    u_raw = [put(f"u_raw{b}", [P, KT, GC * P], F32, L0 + 16384 * b) for b in range(2)]
    L1 = L0 + 32768
    u_hi = [put(f"u_hi{b}", [P, KT, GC * P], BF16, L1 + 16384 * b) for b in range(2)]
    u_lo = [put(f"u_lo{b}", [P, KT, GC * P], BF16, L1 + 8192 + 16384 * b) for b in range(2)]
    L2 = L1 + 32768
    v_raw = [put(f"v_raw{b}", [P, GC, D], F32, L2 + 16384 * b) for b in range(2)]
    L3 = L2 + 32768
    v_hi = [put(f"v_hi{b}", [P, GC, D], BF16, L3 + 16384 * b) for b in range(2)]
    v_lo = [put(f"v_lo{b}", [P, GC, D], BF16, L3 + 8192 + 16384 * b) for b in range(2)]
    L4 = L3 + 32768
    g_in = [put(f"g_in{b}", [P, NBLK, GC, TB], F32, L4 + 8320 * b) for b in range(2)]
    L5 = L4 + 16640
    w_hi = [put(f"w_hi{b}", [P, GC, NT], BF16, L5 + 8320 * b) for b in range(2)]
    w_lo = [put(f"w_lo{b}", [P, GC, NT], BF16, L5 + 4160 + 8320 * b) for b in range(2)]
    L6 = L5 + 16640
    act_f = [put(f"act_f{b}", [P, NT], F32, L6 + 2080 * b) for b in range(2)]
    w_f = [put(f"w_f{b}", [P, NT], F32, L6 + 4160 + 2080 * b) for b in range(2)]
    assert L6 + 8320 <= nc.sbuf_usable_end, (L6 + 8320 - nc.sbuf_usable_end)
    T0 = L2 + 16384
    stage = [put(f"stage{b}", [P, NKEYS, TB], F32, T0 + 20480 * b) for b in range(2)]
    T1 = T0 + 40960
    oneR = [put(f"oneR{b}", [P, 2, P, 4], BF16, T1 + 2048 * b) for b in range(PAIRS)]
    T2 = T1 + 2048 * PAIRS
    gateL = [put(f"gateL{b}", [P, 2, 2, P, 4], BF16, T2 + 4096 * b) for b in range(PAIRS)]
    T3 = T2 + 4096 * PAIRS
    oneL = [put(f"oneL{b}", [P, 2, P, 4], BF16, T3 + 2048 * b) for b in range(2)]
    T4 = T3 + 4096
    keys4 = put("keys4", [P, P, 4], BF16, T4)
    cur = [put(f"cur{b}", [P, 4, TB], BF16, T4 + 1024 + 320 * b) for b in range(2)]
    assert T4 + 1664 <= nc.sbuf_usable_end
    gbank = bank[0:5]
    abank = [pa[:, 2 * b:2 * b + 2, :] for b in range(2)]
    bbank = [pa[:, 4 + 2 * b:6 + 2 * b, :] for b in range(2)]

    d_qk = nc.dram_tensor("d_qk", (2, DB, WID), F32).ap()
    d_v = nc.dram_tensor("d_v", (DB, WID), F32).ap()
    d_g = nc.dram_tensor("d_g", (2, DB, H), F32).ap()
    d_new = nc.dram_tensor("d_new", (DB, H), F32).ap()
    d_h = nc.dram_tensor("d_h", (P, 32), F32).ap()
    d_gate = nc.dram_tensor("d_gate", (NBLK, P, NKEYS, TB), F32).ap()

    def sems(names):
        return [sem(n) for n in names.split()]

    x_in = [sem(f"x_in{k}") for k in range(KT)]
    const_in, sel_in, wg_in, cst_in, sk_in = sems("const_in sel_in wg_in cst_in sk_in")
    w_in = [sem(f"w_in{b}") for b in range(2)]
    kv_in = [sem(f"kv_in{b}") for b in range(NKV)]
    dve, act_o, pool_o = sems("dve_order act_order pool_order")
    ones_set, sq_done, h_done, ax_done, ln_done, lf_done, m_done, enm_done = sems(
        "ones_set sq_done h_done ax_done ln_done lf_done m_done enm_done")
    conv_done, silu_done, kscaled, conv_out = sems("conv_done silu_done kscaled conv_out")
    rope_done, new_done, kp_out, vp_out, m_out = sems("rope_done new_done kp_out vp_out m_out")
    att_scored, att_exp, att_pv, att_out = sems("att_scored att_exp att_pv att_out")
    ml_diag, ml_exp, ml_wk, ml_norm = sems("ml_diag ml_exp ml_wk ml_norm")
    scr_g, scr_qk, scr_v, scr_new, scr_h = sems("scr_g scr_qk scr_v scr_new scr_h")
    sml_in, ss_in, h4_in, c_in = sems("sml_in ss_in h4_in c_in")
    k_used, s_neg, s_exp, s_prob, v_used, d_summed, s_mixed = sems(
        "k_used s_neg s_exp s_prob v_used decode_summed s_mixed")
    ms_ready, ms_exp, ms_h, ms_C, ms_out, Cp_out = sems("ms_ready ms_exp ms_h ms_C ms_out Cp_out")
    sq2_done, h2_done, hs_done = sems("sq2_done h2_done hs_done")
    g_sub, g_exp, tb_done, tb_high = sems("g_sub g_exp tb_done tb_high")
    qz_zero, s_used, rank_steps, one_hot, looked = sems("qz_zero scores_used rank_steps one_hot_ranks looked_up")
    keys_set, cur_done, gl_one, gl_L, gl_R, gl_mm, gl_ev = sems("keys_set cur_done gl_one gl_L gl_R gl_mm gl_ev")
    g_stored = [sem(f"g_stored{b}") for b in range(2)]
    u_in, v_in, gg_in = ([sem(f"{n}{b}") for b in range(2)] for n in ("u_in", "v_in", "gg_in"))
    uhi_done, ulo_done, vhi_done, vlo_done = sems("uhi_done ulo_done vhi_done vlo_done")
    a_made, a_gelu, w_prod, whi_done, wlo_done, b_made, b_added = sems(
        "a_made a_gelu w_prod whi_done wlo_done b_made b_added")
    y_out = sem("y_out")
    CONV_OUT, KP_OUT, VP_OUT, MS_OUT, CP_OUT, SML_IN = 3 * 16, (NPT + 1) * 16, (NPT + 1) * 16, 3 * 16, 2 * 16, 9 * 16

    class Ordered:

        def __init__(self, eng, order):
            self.eng, self.order, self.count = eng, order, {}

        def __call__(self, ins, signal=None):
            s = signal or self.order
            self.count[s.name] = self.count.get(s.name, 0) + 1
            ins.then_inc(s, 1)
            self.eng.wait_ge(s, self.count[s.name])

        def release(self, ins, key):
            release(ins, key)
            emptied(self.eng, key)

    class Group:

        def __init__(self, i, b):
            self.i, self.b, self.n = i + b // 2, b % 2, (i + b // 2) * 2 + b % 2

        def plus(self, k):
            return Group(self.i, self.b + k)

    def wait_pos(eng, s, v):
        if not isinstance(v, int) or v > 0:
            eng.wait_ge(s, v)

    def groups(eng, step):
        for b in range(2):
            step(Group(0, b), False)
        with eng.Fori(1, NG // 2 - 1) as i:
            for b in range(2):
                step(Group(i, b), False)
        for b in range(2):
            step(Group(NG // 2 - 1, b), True)

    def blocks(eng, step, between=None):
        step(0, 0, 0)
        step(1, 1, 0)
        step(2, 0, 1)
        if between:
            between()
        with eng.Fori(1, (NBLK - 1) // 2) as i:
            step(i * 2 + 1, 1, i)
            step(i * 2 + 2, 0, i + 1)

    ATT = [(i, h) for i in range(NPT) for h in range(H)]
    UNITS = [(h, i, P) for h in range(H) for i in range(NPT)] + [(H, NPT, DB * H)]
    TILE = [(P, H * TOPK)] * NPT + [(DB * H, TOPK)]
    LASTS = {"mqk0": ("mqk", 3, 1), "mqk1": ("mqk", 7, 1), "wo0": ("wo", 3, 1), "wo1": ("wo", 7, 1)}
    LASTS.update({g: (g, NTT - 1) for g in ("q", "k", "v", "mo")}, mv=("mv", NPT - 1))
    LASTS.update({f"wq{g}": ("wq", 4 * g + 3, 1) for g in range(4)})

    def weights_arrived(eng, group):
        n = WGROUPS.index(group)
        eng.wait_ge(w_in[n % 2], 16 * (n // 2 + 1))
        return wr[n % 2]

    block = nc.Block()
    with nc.allow_non_contiguous_dma(reason="a few hundred small elements of the decode batch"), block as blk:

        @blk.sync
        def _(sp):
            sp.dma_start(const[:, :], I["const"]).then_inc(const_in, 16)
            sp.dma_start(par[:, :], I["par"]).then_inc(const_in, 16)
            for k in range(KT):
                sp.dma_start(xT[:, k, :], I["xT"][:, k, :]).then_inc(x_in[k], 16)
            sp.dma_start(wg[:, :, :], I["wg"]).then_inc(wg_in, 16)
            def load_weights(n):
                if n >= 2:
                    arrived(sp, LASTS[WGROUPS[n - 2]])
                sp.dma_start(wr[n % 2][:, :, :], I["w"][n]).then_inc(w_in[n % 2], 16)

            def load_cache(m):
                if m >= NKV:
                    if m - NKV < DB:
                        sp.wait_ge(k_used, m - NKV + 1)
                    else:
                        sp.wait_ge(v_used, m - NKV - DB + 1)
                b, cache = m % DB, I["ck"] if m < DB else I["cv"]
                for g3, (_, dil) in enumerate(DIL):
                    sp.dma_start(kv[m % NKV][:, g3, :],
                                 cache[b, NCACHE - P * dil:NCACHE:dil, :]).then_inc(kv_in[m % NKV], 16)

            for n in range(5):
                load_weights(n)
            sp.wait_ge(conv_done, 8)
            sp.wait_ge(conv_out, CONV_OUT)
            load_cache(0)
            load_cache(1)
            load_weights(5)
            load_weights(6)
            for m in range(2, DB + 6):
                load_cache(m)
            sp.wait_ge(ms_h, 1)
            sp.dma_start(d_h, sml[:, 170:202]).then_inc(scr_h, 16)
            sp.wait_ge(ms_C, 1)
            sp.dma_start(O["Cs"], Cs[:, :, :]).then_inc(ms_out, 16)
            sp.dma_start(O["ns"], sml[0:P:2, 256:320]).then_inc(ms_out, 16)
            sp.dma_start(O["ms"], sml[0:P:2, 320:321]).then_inc(ms_out, 16)
            load_cache(DB + 6)
            load_cache(DB + 7)
            for n in range(7, len(WGROUPS)):
                load_weights(n)
                if n == 9:
                    sp.dma_start(skT[:, :, :], I["sk"]).then_inc(sk_in, 16)
            def load_u(g):
                wait_pos(sp, ulo_done, (g.n - 1) * 4)
                sp.dma_start(u_raw[g.b][:, :, :].rearrange("p k e -> p (k e)"),
                             I["uT"][bass.ds(g.n, 1)].rearrange("a p e -> p (a e)")).then_inc(u_in[g.b], 16)

            def load_v(g):
                wait_pos(sp, vlo_done, (g.n - 1) * 4)
                sp.dma_start(v_raw[g.b][:, :, :].rearrange("p k e -> p (k e)"),
                             I["v"][bass.ds(g.n, 1)].rearrange("a p e -> p (a e)")).then_inc(v_in[g.b], 16)

            def load_gates(g):
                wait_pos(sp, w_prod, (g.n - 1) * GC)
                sp.dma_start(g_in[g.b][:, :, :, :],
                             d_gate[:, :, bass.ds(g.n * GC, GC), :].rearrange("a p e t -> p a e t")
                             ).then_inc(gg_in[g.b], 16)

            first = Group(0, 0)
            sp.wait_ge(keys_set, 1)
            load_u(first)
            load_u(first.plus(1))
            load_v(first)

            def store(n, b, i):
                sp.wait_ge(gl_ev, (n + 1) * QUADS)
                sp.dma_start(d_gate[bass.ds(n, 1)].rearrange("a p e t -> p (a e t)"),
                             stage[b][:, :, :].rearrange("p e t -> p (e t)")).then_inc(g_stored[b], 16)

            blocks(sp, store)
            sp.wait_ge(g_stored[0], 16 * (NBLK // 2 + 1))
            sp.wait_ge(g_stored[1], 16 * (NBLK // 2))

            def load(g, last):
                if not (isinstance(g.n, int) and g.n < 2):
                    load_u(g)
                load_gates(g)
                if not (isinstance(g.n, int) and g.n < 1):
                    load_v(g)

            groups(sp, load)
            for m in range(KT):
                sp.wait_ge(b_added, (NG - 1) * KT + m + 1)
                sp.dma_start(O["yT"][:, m, :], xT[:, m, :]).then_inc(y_out, 16)
            sp.wait_ge(y_out, 16 * KT)

        @blk.gpsimd
        def _(pool):
            pool.dma_start(sel[:, :, :], I["sel"]).then_inc(sel_in, 16)
            pool.dma_start(cst[:, :, :, :], I["cst"]).then_inc(cst_in, 16)
            pool.wait_ge(cst_in, 16)
            pool.dma_start(O["convs"][:, :, 0:2, :], cst[:, :, 1:3, :]).then_inc(conv_out, 16)
            for c in range(8):
                for f in range(2):
                    emptied(pool, ("mqk", c, f))
            pool.dma_start(O["convs"][:, :, 2, :], mqkT[:, :, SEQ:NT]).then_inc(conv_out, 16)
            pool.dma_start(O["convp"], mqkT[:, :, SEQ - 3:SEQ]).then_inc(conv_out, 16)
            pool.wait_ge(lf_done, 1)
            pool.dma_start(d_g[0].rearrange("b h -> h b"), ig[:, SEQ:NT]).then_inc(scr_g, 16)
            pool.dma_start(d_g[1].rearrange("b h -> h b"), lf[:, SEQ:NT]).then_inc(scr_g, 16)
            pool.wait_ge(m_done, 1)
            pool.dma_start(O["mp"], mrow[:, SEQ - 1:SEQ]).then_inc(m_out, 16)
            pool.wait_ge(h_done, KT)
            pool.dma_start(Cs[:, :, :], I["C0"]).then_inc(c_in, 16)
            emptied(pool, ("sq",))
            emptied(pool, ("sk",))
            for t in range(2):
                pool.dma_start(d_qk[t], qks[t][:, :]).then_inc(scr_qk, 16)
            emptied(pool, ("mv", NPT))
            pool.dma_start(d_v.rearrange("b (h d) -> b h d", h=H), mv1[0:DB, NPT, :, 0:DH]).then_inc(scr_v, 16)
            pool.wait_ge(new_done, 1)
            pool.dma_start(d_new, st[0:DB, 184:192]).then_inc(scr_new, 16)
            pool.wait_ge(scr_g, 32)
            pool.wait_ge(scr_qk, 32)
            for half in range(2):
                for t in range(2):
                    pool.dma_start(sml[half:P:2, t * DH:(t + 1) * DH],
                                   d_qk[t].rearrange("b (h d) -> (b h) d", h=H)).then_inc(sml_in, 16)
                for t in range(2):
                    pool.dma_start(sml[half:P:2, 160 + t:161 + t],
                                   d_g[t].rearrange("b (h o) -> (b h) o", o=1)).then_inc(sml_in, 16)
            pool.wait_ge(scr_v, 16)
            pool.dma_start(sml[:, 128:160], d_v.rearrange("b (x v) -> (b x) v", v=32)).then_inc(sml_in, 16)
            pool.wait_ge(scr_new, 16)
            pool.wait_ge(conv_done, 8)
            pool.wait_ge(conv_out, CONV_OUT)
            pool.dma_start(SS[:, 384:385], d_new.rearrange("b (h o) -> (b h) o", o=1)).then_inc(ss_in, 16)
            for i in range(NTT):
                emptied(pool, ("v", i))
            for i in range(NPT):
                pool.dma_start(O["vp"][i], zv[:, i, :]).then_inc(vp_out, 16)
            pool.dma_start(O["vs"], zv[0:DB, NPT, :]).then_inc(vp_out, 16)
            pool.wait_ge(rope_done, 2 * NTT)
            for i in range(NPT):
                pool.dma_start(O["kp"][i], zk[:, i, :]).then_inc(kp_out, 16)
            pool.dma_start(O["ks"], zk[0:DB, NPT, :]).then_inc(kp_out, 16)
            pool.wait_ge(scr_h, 16)
            pool.wait_ge(v_used, DB)
            pool.dma_start(hraw[0:DB, NPT, :], d_h.rearrange("(b x) v -> b x v", b=DB)).then_inc(h4_in, 16)
            for h in range(H):
                emptied(pool, ("C", h))
            pool.dma_start(O["Cp"].rearrange("h v k -> v h k"), Cst[0:DH, :, :]).then_inc(Cp_out, 16)
            pool.dma_start(O["np"], Cst[DH:DH + 1, :, :]).then_inc(Cp_out, 16)
            arrived(pool, ("wo", 7, 1))
            pool.memset(qz[:, :, :, :], 0.0)
            pool.memset(qzsq[:, :, :, :], 0.0).then_inc(qz_zero, 1)
            for s, v in ((m_out, 16), (vp_out, VP_OUT), (kp_out, KP_OUT), (Cp_out, CP_OUT), (ms_out, MS_OUT)):
                pool.wait_ge(s, v)

            for u, (h, i, r) in enumerate(UNITS):
                P4 = lambda x: x.then_inc(pool_o, 1)
                pool.wait_ge(one_hot, u + 1)
                P4(pool.tensor_copy(ixf[0:r, :, :], ixs[u % 4][0:r, :, :]))
                pool.wait_ge(pool_o, 5 * u + 1)
                P4(pool.tensor_tensor(picked[0:r], eq[u % 2][0:r], ixf[0:r, :, :].unsqueeze(3).to_broadcast(
                    [r, 2, TOPK, TOPK]), ALU.mult))
                for n, (src, dst) in enumerate(((picked, fold8), (fold8, fold4), (fold4, fold2))):
                    w = 8 >> n
                    pool.wait_ge(pool_o, 5 * u + 2 + n)
                    P4(pool.tensor_tensor(dst[0:r], src[0:r, :, 0:w, :], src[0:r, :, w:2 * w, :], ALU.add))
                pool.wait_ge(pool_o, 5 * u + 5)
                pool.tensor_tensor(idx[0:r, i, :, (h % H) * TOPK:(h % H + 1) * TOPK], fold2[0:r, :, 0, :],
                                   fold2[0:r, :, 1, :], ALU.add).then_inc(looked, 1)
                pool.wait_ge(looked, u + 1)

            first = Group(0, 0)
            for g in (first, first.plus(1)):
                for s in range(4):
                    pool.wait_ge(uhi_done, g.n * 4 + s + 1)
                    pool.tensor_tensor(u_lo[g.b][:, 2 * s:2 * s + 2, :], u_raw[g.b][:, 2 * s:2 * s + 2, :],
                                       u_hi[g.b][:, 2 * s:2 * s + 2, :], ALU.subtract).then_inc(ulo_done, 1)
            for s in range(4):
                pool.wait_ge(vhi_done, s + 1)
                pool.tensor_tensor(v_lo[0][:, s, :], v_raw[0][:, s, :], v_hi[0][:, s, :], ALU.subtract
                                   ).then_inc(vlo_done, 1)

        @blk.scalar
        def _(act):
            A = act.activation

            def copy(key, dst, src):
                release(A(dst, src, ACT.Copy), key)

            for c in range(8):
                for f in range(2):
                    bk = arrived(act, ("mqk", c, f))
                    copy(("mqk", c, f), mqkT[:, c, f * HALF:(f + 1) * HALF], bk[:, 0:HALF])
            act.wait_ge(ax_done, 1)
            A(lfm[:, :], ax[:, :], ACT.Exp, scale=-1.0).then_inc(act_o, 1)
            act.wait_ge(act_o, 1)
            A(lfm[:, :], lfm[:, :], ACT.Ln, bias=1.0).then_inc(ln_done, 1)
            for g, dst in (("q", zq), ("k", zk)):
                for i in range(NTT):
                    bk = arrived(act, (g, i))
                    copy((g, i), dst[0:rows(i), i, :], bk[0:rows(i), :])
            for c in range(8):
                act.wait_ge(conv_done, c + 1)
                A(qkT[:, c, :], qkT[:, c, :], ACT.Silu).then_inc(silu_done, 1)
            act.wait_ge(m_done, 1)
            A(enm[:, :], mrow[:, 0:SEQ], ACT.Exp, scale=-1.0).then_inc(enm_done, 1)
            for i in range(NTT):
                bk = arrived(act, ("v", i))
                copy(("v", i), zv[0:rows(i), i, :], bk[0:rows(i), :])

            def mlstm_v(i):
                bk = arrived(act, ("mv", i))
                copy(("mv", i), mv1[0:rows(i), i, :, 0:DH], bk[0:rows(i), :].rearrange("p (h d) -> p h d", h=H))

            def output_gate(i):
                bk = arrived(act, ("mo", i))
                release(A(sgo[0:rows(i), i, :], bk[0:rows(i), :], ACT.Sigmoid), ("mo", i))

            mlstm_v(NPT)
            act.wait_ge(conv_out, CONV_OUT)
            for n, key in enumerate((("sq",), ("sk",))):
                bk = arrived(act, key)
                copy(key, qks[n][:, :], bk[0:DB, :])
            for i in range(NPT):
                mlstm_v(i)
            output_gate(0)
            act.wait_ge(s_neg, 1)
            A(SS[:, :], SS[:, :], ACT.Exp, bias=st[0:64, 141:142], accum_out=st[0:64, 142:143]).then_inc(s_exp, 1)
            act.wait_ge(ms_ready, 1)
            A(sml[:, 166:169], sml[:, 163:166], ACT.Exp).then_inc(ms_exp, 1)
            for i in range(1, NTT):
                output_gate(i)
            arrived(act, ("mo", NTT - 1))
            for i in range(NPT):
                for g, dst in (("qT", qT), ("kT", kT)):
                    bk = arrived(act, (g, i))
                    copy((g, i), dst[:, :, i * P:(i + 1) * P], bk[:, :].rearrange("p (c t) -> p c t", c=4))
            for n, (i, h) in enumerate(ATT):
                act.wait_ge(att_scored, n + 1)
                if n >= 3:
                    arrived(act, ("PT", *ATT[n - 3]))
                if h == 0 and i >= 2:
                    act.wait_ge(att_out, i - 1)
                A(Pb[n % 3][:, 0:(i + 1) * P], Sb[n % 3][:, 0:(i + 1) * P], ACT.Exp,
                  bias=st[:, 315 + n % 3:316 + n % 3],
                  accum_out=st[:, 20 + 8 * (i % 2) + h:21 + 8 * (i % 2) + h]).then_inc(att_exp, 1)
            bk = arrived(act, ("aT",))
            copy(("aT",), st[:, 48:112], bk[:, 0:64])
            act.wait_ge(kp_out, KP_OUT)
            for i in range(NPT):
                bk = arrived(act, ("kt", i))
                copy(("kt", i), ktok[:, i, :], bk[:, :])
            act.wait_ge(vp_out, VP_OUT)

            def decay(h):
                b = h % 2
                bk = arrived(act, ("nM", h))
                act.wait_ge(ml_diag, h + 1)
                if h >= 2:
                    act.wait_ge(ml_wk, NPT * (h - 1))
                for j in range(NPT - 1):
                    ins = A(Dm[b][:, OJ[j] + P:OJ[j] + (NPT - j) * P], bk[:, (j + 1) * P:SEQ], ACT.Exp,
                            bias=st[:, 48 + j * H + h:49 + j * H + h])
                    if j == NPT - 2:
                        release(ins, ("nM", h))
                for j in range(NPT):
                    ins = A(Dm[b][:, OJ[j]:OJ[j] + P], dm[:, j, :], ACT.Exp,
                            bias=st[:, 48 + j * H + h:49 + j * H + h])
                ins.then_inc(ml_exp, 1)

            emptied(act, ("aT",))
            act.wait_ge(att_out, NPT)
            decay(0)
            for h in range(H):
                if h + 1 < H:
                    decay(h + 1)
                bk = arrived(act, ("C", h))
                copy(("C", h), Cst[:, h, :], bk[0:DH + 1, 0:DH])
            for i in range(NPT):
                bk = arrived(act, ("mA", i))
                copy(("mA", i), mixT[:, 0:4, i * P:(i + 1) * P], bk[:, :].rearrange("p (c t) -> p c t", c=4))
            for i in range(NTT):
                r = rows(i)
                bk = arrived(act, ("mM", i))
                copy(("mM", i), mixT[:, 4:8, i * P:i * P + r],
                     bk[:, 0:4 * r].rearrange("p (c t) -> p c t", c=4))
            def queries(h):
                if h >= 2:
                    arrived(act, ("sc", h - 2, NPT - 1))
                for a in range(2):
                    m, gain = 2 * h + a, par[:, P_GQN + a:P_GQN + a + 1]
                    for f in range(2):
                        bk = arrived(act, ("wq", m, f))
                        A(qg[h % 2][:, a, f * HALF:(f + 1) * HALF], bk[:, 0:HALF], ACT.Identity, scale=gain)
                        if f == 1:
                            A(qz[:, a, h, h:64:H], bk[:, HALF - DB:HALF], ACT.Identity, scale=gain)
                            A(qzsq[:, a, h, h:64:H], bk[:, HALF - DB:HALF], ACT.Square)
                        release(A(qsq[h % 2][:, a, f * HALF:(f + 1) * HALF], bk[:, 0:HALF], ACT.Square), ("wq", m, f))

            def scores_out(u):
                h, i, r = UNITS[u]
                bk = arrived(act, ("sc", h, i))
                if u >= 3:
                    act.wait_ge(s_used, u - 2)
                col = i * H + h % H
                A(nv[0:r, col:col + 1], bk[0:r, 256:257], ACT.Copy)
                release(A(Ssb[u % 3][0:r, :, :], bk[0:r, 0:256].rearrange("p (a n) -> p a n", a=2), ACT.Copy),
                        ("sc", h, i))

            act.wait_ge(qz_zero, 1)
            for h in range(H):
                for g in queries_before(h):
                    queries(g)
                for i in range(NPT):
                    scores_out(h * NPT + i)
            scores_out(H * NPT)
            for i in range(NTT):
                r, n = TILE[i]
                act.wait_ge(g_sub, i + 1)
                A(gt[0:r, i, 0:n], gt[0:r, i, 0:n], ACT.Exp).then_inc(g_exp, 1)

            def evacuate(n, b, i):
                wait_pos(act, g_stored[b], 16 * i)
                for q in range(QUADS):
                    act.wait_ge(gl_mm, n * QUADS + q + 1)
                    A(stage[b][:, :, 4 * q:4 * q + 4],
                      gbank[q % 5][:, :].rearrange("p (t e) -> p e t", t=4), ACT.Copy).then_inc(gl_ev, 1)

            def u_high(g):
                act.wait_ge(u_in[g.b], (g.i + 1) * 16)
                wait_pos(act, a_made, (g.n - 1) * GC)
                for s in range(4):
                    A(u_hi[g.b][:, 2 * s:2 * s + 2, :], u_raw[g.b][:, 2 * s:2 * s + 2, :], ACT.Copy
                      ).then_inc(uhi_done, 1)

            def v_high(g):
                act.wait_ge(v_in[g.b], (g.i + 1) * 16)
                wait_pos(act, b_made, (g.n - 1) * KT)
                for s in range(4):
                    A(v_hi[g.b][:, s, :], v_raw[g.b][:, s, :], ACT.Copy).then_inc(vhi_done, 1)

            def gelu(g):
                for c in range(GC):
                    u = g.n * GC + c
                    act.wait_ge(a_made, u + 1)
                    wait_pos(act, w_prod, u - 1)
                    A(act_f[c % 2][:, :].rearrange("p (f t) -> p f t", f=2), abank[c % 2][:, :, 0:HALF], ACT.Gelu
                      ).then_inc(a_gelu, 1)

            def act_step(g, last):
                more = not (last and g.b == 1)
                if more:
                    gelu(g.plus(1))
                if not last:
                    u_high(g.plus(2))
                if more:
                    v_high(g.plus(1))

            first = Group(0, 0)

            def first_high():
                u_high(first)
                u_high(first.plus(1))

            blocks(act, evacuate, first_high)
            act.wait_ge(g_stored[0], 16 * (NBLK // 2 + 1))
            act.wait_ge(g_stored[1], 16 * (NBLK // 2))
            v_high(first)
            gelu(first)
            groups(act, act_step)

        @blk.vector
        def _(v):
            do = Ordered(v, dve)
            tt, ts, stt = v.tensor_tensor, v.tensor_scalar, v.scalar_tensor_tensor

            def inv_sqrt(y, x, t):
                do(ts(t.bitcast(U32), x.bitcast(U32), 1, None, ALU.logical_shift_right))
                do(ts(y.bitcast(U32), t.bitcast(U32), -1.0, float(0x5F3759DF), ALU.mult, ALU.add))
                for _ in range(3):
                    do(tt(t, y, y, ALU.mult))
                    do(stt(t, t, -0.5, x, ALU.mult, ALU.mult))
                    do(stt(y, t, 1.5, y, ALU.add, ALU.mult))


            def head_stat(src, tmp, i):
                r = rows(i)
                do(tt(tmp[0:r, :], src, src, ALU.mult))
                do(v.tensor_reduce(nv[0:r, i * H:(i + 1) * H], tmp[0:r, :].rearrange("p (h d) -> p h d", h=H),
                                   AX.X, ALU.add))

            def inv_rms(n):
                do(ts(nv, nv, 1.0 / n, EPS, ALU.mult, ALU.add))
                inv_sqrt(ny, nv, na)

            do(v.memset(ones[:, :], 1.0), ones_set)
            do(v.memset(ones_row[:, :], 1.0))
            do(v.memset(nv, 1.0))
            for i in range(NTT):
                do(v.memset(mv1[:, i, :, DH:DH + 1], 1.0))
            v.wait_ge(const_in, 32)
            for k in range(KT):
                v.wait_ge(x_in[k], 16)
                do(tt(sqT[:, k, :], xT[:, k, :], xT[:, k, :], ALU.mult), sq_done)
            for f in range(2):
                bk = arrived(v, ("n1", f))
                do.release(ts(msq[:, f * HALF:(f + 1) * HALF], bk[:, 0:HALF], 1.0 / D, EPS, ALU.mult, ALU.add),
                           ("n1", f))
            inv_sqrt(rstd[:, :], msq[:, :], mtmp[:, :])
            for k in range(KT):
                do(stt(hT[:, k, :], xT[:, k, :], par[:, P_G1 + k:P_G1 + k + 1], rstd[:, :], ALU.mult, ALU.mult),
                   h_done)
            for n, (g, dst) in enumerate((("gi", ig), ("gf", fx))):
                for f in range(2):
                    bk = arrived(v, (g, f))
                    do.release(ts(dst[:, f * HALF:(f + 1) * HALF], bk[0:H, 0:HALF],
                                  par[0:H, P_BG8 + n:P_BG8 + n + 1], None, ALU.add), (g, f))
            do(stt(ax[:, :], fx[:, :], -1.0, fx[:, :], ALU.mult, ALU.max), ax_done)
            do(ts(fx[:, :], fx[:, :], 0.0, None, ALU.min))
            v.wait_ge(ln_done, 1)
            do(tt(lf[:, :], fx[:, :], lfm[:, :], ALU.subtract), lf_done)
            do(v.tensor_tensor_scan(cumB[:, 0:SEQ], ones_row[:, :], lf[:, 0:SEQ], 0.0, ALU.mult, ALU.add))
            do(tt(arow[:, :], ig[:, 0:SEQ], cumB[:, 0:SEQ], ALU.subtract))
            do(v.tensor_tensor_scan(nrow[:, 0:SEQ], ones_row[:, :], arow[:, :], 0.0, ALU.mult, ALU.max))
            do(tt(mrow[:, 0:SEQ], cumB[:, 0:SEQ], nrow[:, 0:SEQ], ALU.add), m_done)
            do(ts(nrow[:, 0:SEQ], nrow[:, 0:SEQ], -1.0, None, ALU.mult))
            v.wait_ge(cst_in, 16)
            for j in range(CW - 1):
                do(tt(convt[:, :, j, :], cst[:, :, j, :],
                      par[:, P_CW:P_CW + 32].rearrange("p (c w) -> p c w", w=4)[:, :, j:j + 1].to_broadcast([P, KT, DB]),
                      ALU.mult))
            for c in range(KT):
                for f in range(2):
                    emptied(v, ("mqk", c, f))
                w = lambda j: par[:, P_CW + 4 * c + j:P_CW + 4 * c + j + 1]
                do(ts(qkT[:, c, :], mqkT[:, c, :], w(3), par[:, P_CB + c:P_CB + c + 1], ALU.mult, ALU.add))
                for j in range(CW - 1):
                    do(tt(qkT[:, c, SEQ:NT], qkT[:, c, SEQ:NT], convt[:, c, j, :], ALU.add))
                for j in (2, 1, 0):
                    s = 3 - j
                    do(stt(qkT[:, c, s:SEQ], mqkT[:, c, 0:SEQ - s], w(j), qkT[:, c, s:SEQ], ALU.mult, ALU.add),
                       conv_done if j == 0 else None)

            def rope(z, i, gain):
                r = rows(i)
                zf = z[0:r, i, :]
                z3 = zf.rearrange("p (h d) -> p h d", h=H)
                t3 = rt[0:r, :].rearrange("p (h d) -> p h d", h=H)
                u3 = rt2[0:r, :].rearrange("p (h d) -> p h d", h=H)
                ss = ny[0:r, i * H:(i + 1) * H]
                do(tt(z3, z3, ss.unsqueeze(2).to_broadcast([r, H, DH]), ALU.mult))
                do(tt(z3, z3, par[0:r, gain:gain + DH].unsqueeze(1).to_broadcast([r, H, DH]), ALU.mult))
                cos = cosT[0:r, i, :].unsqueeze(1).to_broadcast([r, H, 32])
                sin = sinT[0:r, i, :].unsqueeze(1).to_broadcast([r, H, 32])
                do(tt(t3[:, :, 0:32], z3[:, :, 0:32], cos, ALU.mult))
                do(tt(u3[:, :, 0:32], z3[:, :, 32:64], sin, ALU.mult))
                do(tt(t3[:, :, 32:64], z3[:, :, 0:32], sin, ALU.mult))
                do(tt(u3[:, :, 32:64], z3[:, :, 32:64], cos, ALU.mult))
                do(tt(z3[:, :, 0:32], t3[:, :, 0:32], u3[:, :, 0:32], ALU.subtract))
                do(tt(z3[:, :, 32:64], t3[:, :, 32:64], u3[:, :, 32:64], ALU.add), rope_done)

            for g, z, gain in (("q", zq, P_GQ), ("k", zk, P_GK)):
                for i in range(NTT):
                    emptied(v, (g, i))
                    head_stat(z[0:rows(i), i, :], rt, i)
                inv_rms(DH)
                if g == "q":
                    do(ts(ny, ny, DH ** -0.5, None, ALU.mult))
                for i in range(NTT):
                    rope(z, i, gain)
            do(tt(rt[0:DB, :], zq[0:DB, NPT, :], zk[0:DB, NPT, :], ALU.mult))
            do(v.tensor_reduce(st[0:DB, 184:192], rt[0:DB, :].rearrange("p (h d) -> p h d", h=H), AX.X, ALU.add),
               new_done)
            v.wait_ge(silu_done, 8)
            for c in range(4, 8):
                do(ts(qkT[:, c, :], qkT[:, c, :], DH ** -0.5, None, ALU.mult), kscaled)

            for b in range(DB):
                bk = arrived(v, ("qb", b))
                v.wait_ge(kv_in[b % NKV], 48 * (b // NKV + 1))
                do.release(tt(kprod[:, :, :], kv[b % NKV][:, :, :],
                              bk[:, :].unsqueeze(1).to_broadcast([P, 3, WID]), ALU.mult), ("qb", b))
                do(v.tensor_reduce(sSc[:, :, b, :], kprod[:, :, :].rearrange("p g (h d) -> p g h d", h=H),
                                   AX.X, ALU.add), k_used)
            bk = arrived(v, ("sS",))
            do.release(v.tensor_copy(SS[:, 0:384], bk[0:64, 0:384]), ("sS",))
            v.wait_ge(ss_in, 16)
            do(ts(SS[:, 384:385], SS[:, 384:385], math.log(3.0), None, ALU.add))
            do(v.tensor_reduce(st[0:64, 140:141], SS[:, :], AX.X, ALU.max))
            do(ts(st[0:64, 141:142], st[0:64, 140:141], -1.0, None, ALU.mult), s_neg)
            v.wait_ge(sml_in, SML_IN)
            v.wait_ge(c_in, 16)
            q_, k_, v_ = sml[:, 0:64], sml[:, 64:128], sml[:, 128:160]
            col = lambda n: sml[:, n:n + 1]
            n0 = par[:, P_N0:P_N0 + DH]
            do(tt(col(162), col(161), par[:, P_M0:P_M0 + 1], ALU.add))
            do(tt(col(320), col(162), col(160), ALU.max))
            do(tt(col(163), col(162), col(320), ALU.subtract))
            do(tt(col(164), col(160), col(320), ALU.subtract))
            do(ts(col(165), col(320), -1.0, None, ALU.mult), ms_ready)
            scale, gain, floor = col(166), col(167), col(168)
            bc_k = lambda x: x.unsqueeze(1).to_broadcast([P, 32, DH])
            do(v.tensor_tensor_reduce(sml[:, 330:394], q_, k_, 1.0, 0.0, ALU.mult, ALU.add, col(234)))
            do(v.tensor_tensor_reduce(sml[:, 330:394], q_, n0, 1.0, 0.0, ALU.mult, ALU.add, col(235)))
            do(tt(Ct[:, :, :], Cs[:, :, :], bc_k(q_), ALU.mult))
            do(v.tensor_reduce(sml[:, 202:234], Ct[:, :, :], AX.X, ALU.add))
            v.wait_ge(s_exp, 1)
            do(v.reciprocal(st[0:64, 143:144], st[0:64, 142:143]))
            do(ts(SS[:, :], SS[:, :], st[0:64, 143:144], None, ALU.mult))
            do(ts(dP[:, :], ident[0:64, 0:64], SS[:, 384:385], None, ALU.mult), s_prob)
            bk = arrived(v, ("sP",))
            do(v.tensor_copy(PTs[:, :], bk[:, 0:192]))
            do.release(v.tensor_copy(Pd[:, :], bk[0:DB, 192:256]), ("sP",))
            v.wait_ge(ms_exp, 1)
            do(tt(col(236), col(234), gain, ALU.mult))
            do(ts(sml[:, 202:234], sml[:, 202:234], scale, None, ALU.mult))
            do(stt(sml[:, 170:202], v_, col(236), sml[:, 202:234], ALU.mult, ALU.add))
            do(ts(col(237), col(235), scale, col(236), ALU.mult, ALU.add))
            do(stt(col(237), col(237), -1.0, col(237), ALU.mult, ALU.max))
            do(tt(col(237), col(237), floor, ALU.max))
            do(v.reciprocal(col(237), col(237)))
            do(ts(sml[:, 170:202], sml[:, 170:202], col(237), None, ALU.mult), ms_h)
            do(ts(sml[:, 256:320], n0, scale, None, ALU.mult))
            do(stt(sml[:, 256:320], k_, gain, sml[:, 256:320], ALU.mult, ALU.add))
            do(ts(Cs[:, :, :], Cs[:, :, :], scale, None, ALU.mult))
            do(tt(Ct[:, :, :], v_.unsqueeze(2).to_broadcast([P, 32, DH]), bc_k(k_), ALU.mult))
            do(stt(Cs[:, :, :], Ct[:, :, :], gain, Cs[:, :, :], ALU.mult, ALU.add), ms_C)

            v.wait_ge(ms_out, MS_OUT)

            def row_max(n):
                i, h = ATT[n]
                w = (i + 1) * P
                bk = arrived(v, ("S", i, h))
                if n >= 3:
                    v.wait_ge(att_exp, n - 2)
                release(v.tensor_tensor_reduce(Sb[n % 3][:, 0:w], bk[:, 0:w], maskt[:, 384 - i * P:SEQ], 1.0, -3e38,
                                               ALU.add, ALU.max, st[:, 312 + n % 3:313 + n % 3]), ("S", i, h))

            def minus_row_max(n):
                emptied(v, ("S", *ATT[n]))
                ts(st[:, 315 + n % 3:316 + n % 3], st[:, 312 + n % 3:313 + n % 3], -1.0, None, ALU.mult
                   ).then_inc(att_scored, 1)

            def divide(i):
                v.wait_ge(att_pv, H * (i + 1))
                l0 = 20 + 8 * (i % 2)
                do(v.reciprocal(st[:, 36:44], st[:, l0:l0 + 8]))
                do(tt(atok[:, i, :].rearrange("p (h d) -> p h d", h=H),
                      acc[i % 2][:, :].rearrange("p (h d) -> p h d", h=H),
                      st[:, 36:44].unsqueeze(2).to_broadcast([P, H, DH]), ALU.mult), att_out)

            for n in range(2):
                row_max(n)
                minus_row_max(n)
            for n, (i, h) in enumerate(ATT):
                if n + 2 < len(ATT):
                    row_max(n + 2)
                w = (i + 1) * P
                bk = arrived(v, ("PT", i, h))
                if n >= 3:
                    v.wait_ge(att_pv, n - 2)
                release(v.tensor_copy(PTb[n % 3][:, 0:i + 1, :], bk[:, 0:w].rearrange("p (j t) -> p j t", j=i + 1)),
                        ("PT", i, h))
                if n + 2 < len(ATT):
                    minus_row_max(n + 2)
                if n == H:
                    v.wait_ge(v_used, DB)
                    for c in range(4):
                        for half in range(2):
                            ps = slice(64 * half, 64 * half + 64)
                            ins = v.tensor_copy(decT[ps, c, :], acc[1][ps, c * 64 + 2 * c + half:c * 64 + 64:8])
                    do(ins, d_summed)
                if h == 1 and i >= 1:
                    divide(i - 1)
            divide(NPT - 1)

            v.wait_ge(conv_out, CONV_OUT)

            def diagonal(h):
                bk = arrived(v, ("nM", h))
                if h >= 1:
                    v.wait_ge(ml_exp, h)
                do(tt(dm[:, :, :], bk[:, :].rearrange("p (j t) -> p j t", j=NPT),
                      causal.unsqueeze(1).to_broadcast([P, NPT, P]), ALU.add), ml_diag)

            diagonal(0)
            for h in range(H):
                b = h % 2
                if h + 1 < H:
                    diagonal(h + 1)
                v.wait_ge(ml_exp, h + 1)
                if h >= 2:
                    arrived(v, ("num", h - 2))
                    arrived(v, ("C", h - 2))
                for j in range(NPT):
                    w = (NPT - j) * P
                    bk = arrived(v, ("ST", h, j))
                    do.release(tt(sdm[b][:, OJ[j]:OJ[j] + w], bk[:, 0:w], Dm[b][:, OJ[j]:OJ[j] + w], ALU.mult),
                               ("ST", h, j))
                for j in range(NPT):
                    last = OJ[j] + (NPT - j) * P - 1
                    if h == 0:
                        emptied(v, ("kt", j))
                    do(ts(wk[b][:, j, :], ktok[:, j, h * DH:(h + 1) * DH], Dm[b][:, last:last + 1], None, ALU.mult),
                       ml_wk)
                bk = arrived(v, ("num", h))
                num = bk[:, 0:4 * (DH + 1)].rearrange("p (i d) -> p i d", i=NPT)
                den = st[:, 112:116]
                do(v.tensor_copy(den, num[:, :, DH]))
                do(stt(den, den, -1.0, den, ALU.mult, ALU.max))
                do(tt(den, den, st[:, 80 + h:112:H], ALU.max))
                do(v.reciprocal(den, den))
                do.release(tt(hraw[:, 0:NPT, h * DH:(h + 1) * DH], num[:, :, 0:DH],
                              den.unsqueeze(2).to_broadcast([P, NPT, DH]), ALU.mult), ("num", h))

            do(v.tensor_copy(mixT[:, 0:4, SEQ:NT], decT), s_mixed)

            for i in range(NTT):
                if i == NPT:
                    v.wait_ge(h4_in, 16)
                head_stat(hraw[0:rows(i), i, :], ht, i)
            inv_rms(DH)
            for i in range(NTT):
                r = rows(i)
                hr = hraw[0:r, i, :]
                h3 = hr.rearrange("p (h d) -> p h d", h=H)
                ss = ny[0:r, i * H:(i + 1) * H]
                do(tt(h3, h3, ss.unsqueeze(2).to_broadcast([r, H, DH]), ALU.mult))
                do(tt(hr, hr, par[0:r, P_GM:P_GM + WID], ALU.mult))
                emptied(v, ("mo", i))
                do(tt(hr, hr, sgo[0:r, i, :], ALU.mult), ml_norm)

            for m in range(KT):
                for f in range(2):
                    t = slice(f * HALF, (f + 1) * HALF)
                    bk = arrived(v, ("wo", m, f))
                    do.release(tt(xT[:, m, t], xT[:, m, t], bk[:, 0:HALF], ALU.add), ("wo", m, f))
                if m == 0:
                    arrived(v, ("mM", NTT - 1))
                do(tt(sqT[:, m, :], xT[:, m, :], xT[:, m, :], ALU.mult), sq2_done)
            for f in range(2):
                bk = arrived(v, ("n2", f))
                do.release(ts(msq[:, f * HALF:(f + 1) * HALF], bk[:, 0:HALF], 1.0 / D, EPS, ALU.mult, ALU.add),
                           ("n2", f))
            inv_sqrt(rstd2[:, :], msq[:, :], mtmp[:, :])
            for k in range(KT):
                do(stt(hT[:, k, :], xT[:, k, :], par[:, P_G2 + k:P_G2 + k + 1], rstd2[:, :], ALU.mult, ALU.mult),
                   h2_done)
            v.wait_ge(m_out, 16)
            v.wait_ge(scr_g, 32)
            for k in range(KT):
                do(v.tensor_copy(h_hi[:, k, :], hT[:, k, :]))
                do(tt(h_lo[:, k, :], hT[:, k, :], h_hi[:, k, :], ALU.subtract), hs_done)

            v.wait_ge(Cp_out, CP_OUT)

            at = {}

            def step(name, ins):
                at[name] = len(at) + 1
                ins.then_inc(rank_steps, 1)

            def after(name):
                v.wait_ge(rank_steps, at[name])

            do(v.tensor_copy(ranks16[:, :, :], iota[:, 0:TOPK].unsqueeze(2).to_broadcast([P, TOPK, TOPK])))

            def picks_of(tensor, u):
                h, i, r = UNITS[u]
                return tensor[0:r, i, (h % H) * TOPK:(h % H + 1) * TOPK]

            def first8(u, a):
                r = UNITS[u][2]
                step(("first", u, a), v.max(vals[u % 2][0:r, a, 0:8], Ssb[u % 3][0:r, a, :]))

            def index8(u, a):
                r = UNITS[u][2]
                after(("first", u, a))
                step(("index", u, a), v.max_index(ixs[u % 4][0:r, a, 0:8], vals[u % 2][0:r, a, 0:8],
                                                  Ssb[u % 3][0:r, a, :]))

            def strike8(u, a):
                r = UNITS[u][2]
                ins = v.match_replace(rest[0:r, a, :], vals[u % 2][0:r, a, 0:8], Ssb[u % 3][0:r, a, :], LOWEST)
                if a == 0:
                    step(("rest", u, a), ins)
                else:
                    ins.then_inc(s_used, 1)

            def second8(u, a):
                r = UNITS[u][2]
                if a == 0:
                    after(("rest", u, a))
                else:
                    v.wait_ge(s_used, u + 1)
                step(("second", u, a), v.max(vals[u % 2][0:r, a, 8:16], rest[0:r, a, :]))

            def index16(u, a):
                r = UNITS[u][2]
                after(("second", u, a))
                step(("index2", u, a), v.max_index(ixs[u % 4][0:r, a, 8:16], vals[u % 2][0:r, a, 8:16],
                                                   rest[0:r, a, :]))

            def sums(u):
                r = UNITS[u][2]
                after(("second", u, 1))
                step(("sums", u), tt(cand[0:r, :, :], vals[u % 2][0:r, 0, :].unsqueeze(2).to_broadcast([r, TOPK, TOPK]),
                                     vals[u % 2][0:r, 1, :].unsqueeze(1).to_broadcast([r, TOPK, TOPK]), ALU.add))

            def flat(u):
                return cand[0:UNITS[u][2], :, :].rearrange("p a b -> p (a b)")

            def sum_first8(u):
                after(("sums", u))
                step(("sum first", u), v.max(picks_of(SC, u)[:, 0:8], flat(u)))

            def sum_strike8(u):
                after(("sum first", u))
                step(("sum rest", u), v.match_replace(crest[0:UNITS[u][2], :], picks_of(SC, u)[:, 0:8], flat(u), LOWEST))

            def sum_index8(u):
                step(("sum index", u), v.max_index(CI[u % 2][0:UNITS[u][2], 0:8], picks_of(SC, u)[:, 0:8], flat(u)))

            def sum_second8(u):
                after(("sum rest", u))
                step(("sum second", u), v.max(picks_of(SC, u)[:, 8:16], crest[0:UNITS[u][2], :]))

            def sum_index16(u):
                after(("sum second", u))
                step(("sum index2", u), v.max_index(CI[u % 2][0:UNITS[u][2], 8:16], picks_of(SC, u)[:, 8:16],
                                                    crest[0:UNITS[u][2], :]))

            def rank_halves(u):
                r = UNITS[u][2]
                after(("sum index2", u))
                step(("rank1", u), ts(abu[0:r, 0, :], CI[u % 2][0:r, :], 4, None, ALU.logical_shift_right))
                step(("rank2", u), ts(abu[0:r, 1, :], CI[u % 2][0:r, :], 15, None, ALU.bitwise_and))

            def rank_copy(u):
                r = UNITS[u][2]
                after(("rank2", u))
                step(("ranks", u), v.tensor_copy(abf[0:r, :, :], abu[0:r, :, :]))

            def rank_rows(u):
                r = UNITS[u][2]
                after(("ranks", u))
                if u >= 2:
                    v.wait_ge(looked, u - 1)
                tt(eq[u % 2][0:r, :, :, :], abf[0:r, :, :].unsqueeze(2).to_broadcast([r, 2, TOPK, TOPK]),
                   ranks16[0:r, :, :].unsqueeze(1).to_broadcast([r, 2, TOPK, TOPK]), ALU.is_equal).then_inc(one_hot, 1)

            for u in range(len(UNITS) + 2):
                a, c, d = u < len(UNITS), 0 <= u - 1 < len(UNITS), 0 <= u - 2
                if a:
                    emptied(v, ("sc", *UNITS[u][0:2]))
                    if u >= 4:
                        v.wait_ge(looked, u - 3)
                    first8(u, 0)
                    first8(u, 1)
                if c:
                    sums(u - 1)
                if d:
                    rank_halves(u - 2)
                if a:
                    index8(u, 0)
                    strike8(u, 0)
                if d:
                    rank_copy(u - 2)
                if a:
                    index8(u, 1)
                    strike8(u, 1)
                if c:
                    sum_first8(u - 1)
                if d:
                    rank_rows(u - 2)
                if a:
                    second8(u, 0)
                if c:
                    sum_strike8(u - 1)
                if a:
                    second8(u, 1)
                if c:
                    sum_index8(u - 1)
                    sum_second8(u - 1)
                if a:
                    index16(u, 0)
                    index16(u, 1)
                if c:
                    sum_index16(u - 1)

            inv_rms(2 * P)

            def by_head(tensor, i):
                r, n = TILE[i]
                return tensor[0:r, i, 0:n].rearrange("p (h k) -> p h k", k=TOPK)

            def per_head(stat, i):
                r, n = TILE[i]
                return stat[0:r, i * H:i * H + n // TOPK].unsqueeze(2).to_broadcast([r, n // TOPK, TOPK])

            for i in range(NTT):
                sc3 = by_head(SC, i)
                step(("lessmax", i), tt(by_head(gt, i), sc3, sc3[:, :, 0:1].to_broadcast([TILE[i][0], TILE[i][1] // TOPK, TOPK]),
                                        ALU.subtract))
            for i in range(NTT):
                after(("lessmax", i))
                tt(by_head(gt, i), by_head(gt, i), per_head(ny, i), ALU.mult).then_inc(g_sub, 1)
            for i in range(NTT):
                r, n = TILE[i]
                v.wait_ge(g_exp, i + 1)
                step(("total", i), v.tensor_reduce(nv[0:r, i * H:i * H + n // TOPK], by_head(gt, i), AX.X, ALU.add))
            for i in range(NTT):
                r, n = TILE[i]
                after(("total", i))
                step(("share", i), v.reciprocal(nv[0:r, i * H:i * H + n // TOPK], nv[0:r, i * H:i * H + n // TOPK]))
            for i in range(NTT):
                after(("share", i))
                ins = tt(by_head(gt, i), by_head(gt, i), per_head(nv, i), ALU.mult)
                if i < NPT:
                    ins.then_inc(tb_done, 1)
                else:
                    step("decode gates", ins)
            v.wait_ge(looked, len(UNITS))
            after("decode gates")
            for n, src in enumerate((idx[0:64, NPT, 0, 0:TOPK], idx[0:64, NPT, 1, 0:TOPK], gt[0:64, NPT, 0:TOPK])):
                ins = tt(byrow[:, n, :].rearrange("p (h k) -> p h k", h=H), src.unsqueeze(1).to_broadcast([64, H, TOPK]),
                         selh.unsqueeze(2).to_broadcast([64, H, TOPK]), ALU.mult)
            ins.then_inc(tb_done, 1)
            for i in range(NTT):
                r = rows(i)
                bk = arrived(v, ("tb", i))
                t = slice(i * P, i * P + r)
                v.tensor_copy(tables[:, 2, t], bk[:, 2 * r:3 * r]).then_inc(tb_high, 1)
                v.tensor_copy(tables[:, 0, t], bk[:, 0:r])
                v.tensor_copy(tables[:, 1, t], bk[:, r:2 * r])
                v.wait_ge(tb_high, i + 1)
                do.release(tt(tables[:, 3, t], bk[:, 2 * r:3 * r], tables[:, 2, t], ALU.subtract), ("tb", i))

            do(v.tensor_copy(keys4[:, :, :], iota.unsqueeze(2).to_broadcast([P, P, 4])), keys_set)

            def gate_rows(n, b, i):
                wait_pos(v, gl_L, (n - 1) * 2 * PAIRS)
                v.tensor_copy(cur[b][:, :, :], tables[:, :, bass.ds(n * TB, TB)]).then_inc(cur_done, 1)
                v.wait_ge(cur_done, n + 1)
                for p in range(PAIRS):
                    u = n * PAIRS + p
                    each = lambda row: cur[b][:, row, 8 * p:8 * p + 8].rearrange(
                        "p (q t) -> p q t", q=2).unsqueeze(2).to_broadcast([P, 2, P, 4])
                    keys = keys4[:, :, :].unsqueeze(1).to_broadcast([P, 2, P, 4])
                    wait_pos(v, gl_L, (u - 1) * 2)
                    tt(oneL[p % 2][:, :, :, :], keys, each(0), ALU.is_equal).then_inc(gl_one, 1)
                    wait_pos(v, gl_mm, 2 * (u - PAIRS + 1))
                    tt(oneR[p][:, :, :, :], keys, each(1), ALU.is_equal).then_inc(gl_R, 1)
                    v.wait_ge(gl_one, u + 1)
                    for part in range(2):
                        tt(gateL[p][:, part, :, :, :], oneL[p % 2][:, :, :, :], each(2 + part), ALU.mult
                           ).then_inc(gl_L, 1)

            blocks(v, gate_rows)

            def u_low(g, s):
                v.wait_ge(uhi_done, g.n * 4 + s + 1)
                tt(u_lo[g.b][:, 2 * s:2 * s + 2, :], u_raw[g.b][:, 2 * s:2 * s + 2, :],
                   u_hi[g.b][:, 2 * s:2 * s + 2, :], ALU.subtract).then_inc(ulo_done, 1)

            def v_low(g, s):
                v.wait_ge(vhi_done, g.n * 4 + s + 1)
                tt(v_lo[g.b][:, s, :], v_raw[g.b][:, s, :], v_hi[g.b][:, s, :], ALU.subtract).then_inc(vlo_done, 1)

            def gated(g):
                v.wait_ge(gg_in[g.b], (g.i + 1) * 16)
                wait_pos(v, b_made, (g.n - 1) * KT)
                for c in range(GC):
                    u = g.n * GC + c
                    v.wait_ge(a_gelu, u + 1)
                    wf = w_f[c % 2]
                    tt(wf[:, :].rearrange("p (a t) -> p a t", a=NBLK),
                       act_f[c % 2][:, :].rearrange("p (a t) -> p a t", a=NBLK), g_in[g.b][:, :, c, :],
                       ALU.mult).then_inc(w_prod, 1)
                    v.wait_ge(w_prod, u + 1)
                    v.tensor_copy(w_hi[g.b][:, c, :], wf[:, :]).then_inc(whi_done, 1)
                    v.wait_ge(whi_done, u + 1)
                    tt(w_lo[g.b][:, c, :], wf[:, :], w_hi[g.b][:, c, :], ALU.subtract).then_inc(wlo_done, 1)

            def dve_step(g, last):
                more = not (last and g.b == 1)
                if more:
                    gated(g.plus(1))
                for m in range(KT):
                    v.wait_ge(b_made, g.n * KT + m + 1)
                    x3 = xT[:, m, :].rearrange("p (f t) -> p f t", f=2)
                    tt(x3, x3, bbank[m % 2][:, :, 0:HALF], ALU.add).then_inc(b_added, 1)
                    if 1 <= m < 5 and not last:
                        u_low(g.plus(2), m - 1)
                    if m >= 4 and more:
                        v_low(g.plus(1), m - 4)

            v.wait_ge(gl_mm, NBLK * QUADS)
            v.wait_ge(ulo_done, 8)
            v.wait_ge(vlo_done, 4)
            gated(Group(0, 0))
            groups(v, dve_step)

        @blk.tensor
        def _(pe):
            def product(dst, pairs, key=None):
                for n, (l, r) in enumerate(pairs):
                    mm = pe.matmul(dst, l, r, start=(n == 0), stop=(n == len(pairs) - 1))
                if key:
                    made(mm, key)
                return mm

            def turn(dst, src, n):
                return pe.transpose(dst, src, ident[0:n, 0:n])

            halves = [slice(0, HALF), slice(HALF, NT)]
            pe.wait_ge(ones_set, 1)
            pe.wait_ge(const_in, 32)
            for f in range(2):
                bk = claim(pe, ("n1", f))
                if f == 0:
                    pe.wait_ge(sq_done, KT)
                product(bk[:, 0:HALF], [(ones[:, :], sqT[:, k, halves[f]]) for k in range(KT)], ("n1", f))
            pe.wait_ge(h_done, KT)
            pe.wait_ge(wg_in, 16)
            for n, g in enumerate(("gi", "gf")):
                for f in range(2):
                    bk = claim(pe, (g, f))
                    product(bk[0:H, 0:HALF], [(wg[:, k, n * H:(n + 1) * H], hT[:, k, halves[f]]) for k in range(KT)],
                            (g, f))
            for c in range(8):
                w = weights_arrived(pe, f"mqk{c // 4}")
                for f in range(2):
                    bk = claim(pe, ("mqk", c, f))
                    product(bk[:, 0:HALF], [(w[:, k, (c % 4) * P:(c % 4 + 1) * P], hT[:, k, halves[f]])
                                            for k in range(KT)], ("mqk", c, f))
            def token_tile(g, i):
                w, r = weights_arrived(pe, g), rows(i)
                bk = claim(pe, (g, i))
                product(bk[0:r, :], [(hT[:, k, i * P:i * P + r], w[:, k, :]) for k in range(KT)], (g, i))

            for g in ("q", "k", "v"):
                for i in range(NTT):
                    token_tile(g, i)
            token_tile("mv", NPT)
            pe.wait_ge(kscaled, 4)
            for n, key in enumerate((("sq",), ("sk",))):
                bk = claim(pe, key)
                for c in range(4):
                    mm = turn(bk[0:DB, c * P:(c + 1) * P], qkT[:, 4 * n + c, SEQ:NT], P)
                made(mm, key)
            pe.wait_ge(sel_in, 16)
            for i in range(NPT):
                token_tile("mv", i)
                for b in (2 * i, 2 * i + 1):
                    bk = claim(pe, ("qb", b))
                    product(bk[:, :], [(sel[:, b, :], zq[0:DB, NPT, :])], ("qb", b))
            token_tile("mo", 0)
            bk = claim(pe, ("sS",))
            pe.wait_ge(k_used, DB)
            for g in range(3):
                mm = turn(bk[0:64, g * P:(g + 1) * P], sSc[:, g, :, :].rearrange("p b h -> p (b h)"), P)
            made(mm, ("sS",))
            token_tile("mo", 1)
            bk = claim(pe, ("sP",))
            pe.wait_ge(s_prob, 1)
            for g in range(3):
                turn(bk[:, g * 64:(g + 1) * 64], SS[:, g * P:(g + 1) * P], 64)
            product(bk[0:DB, 192:256], [(seld, dP[:, :])], ("sP",))

            def decode_values(b):
                if b == 0:
                    emptied(pe, ("sP",))
                    emptied(pe, ("v", NPT))
                    for c in range(4):
                        pe.matmul(acc[1][:, c * 64:(c + 1) * 64], zv[0:DB, NPT, c * P:(c + 1) * P], Pd[:, :],
                                  start=(c == 0), stop=False, skip_group_check=True)
                m = DB + b
                pe.wait_ge(kv_in[m % NKV], 48 * (m // NKV + 1))
                for g in range(3):
                    for c in range(4):
                        mm = pe.matmul(acc[1][:, c * 64 + b * H:c * 64 + (b + 1) * H],
                                       kv[m % NKV][:, g, c * P:(c + 1) * P], PTs[:, g * 64 + b * H:g * 64 + (b + 1) * H],
                                       start=False, stop=(g == 2), skip_group_check=True)
                mm.then_inc(v_used, 1)

            token_tile("mo", 2)
            decode_values(0)
            decode_values(1)
            token_tile("mo", 3)
            decode_values(2)
            token_tile("mo", 4)
            decode_values(3)
            pe.wait_ge(rope_done, 2 * NTT)
            for i in range(NPT):
                for g, z in (("qT", zq), ("kT", zk)):
                    bk = claim(pe, (g, i))
                    for c in range(4):
                        mm = turn(bk[:, c * P:(c + 1) * P], z[:, i, c * P:(c + 1) * P], P)
                    made(mm, (g, i))
            for i in range(NPT):
                emptied(pe, ("qT", i))
                emptied(pe, ("kT", i))
                emptied(pe, ("v", i))

            def scores(i, h):
                bk = claim(pe, ("S", i, h))
                ps = slice(64 * (h % 2), 64 * (h % 2) + 64)
                product(bk[:, 0:(i + 1) * P], [(qT[ps, h // 2, i * P:(i + 1) * P], kT[ps, h // 2, 0:(i + 1) * P])],
                        ("S", i, h))

            def values(n):
                i, h = ATT[n]
                emptied(pe, ("PT", i, h))
                if h == 0 and i == 1:
                    pe.wait_ge(d_summed, 1)
                if h == 0 and i >= 2:
                    pe.wait_ge(att_out, i - 1)
                product(acc[i % 2][:, h * DH:(h + 1) * DH],
                        [(PTb[n % 3][:, j, :], zv[:, j, h * DH:(h + 1) * DH]) for j in range(i + 1)]
                        ).then_inc(att_pv, 1)

            scores(*ATT[0])
            scores(*ATT[1])
            for n, (i, h) in enumerate(ATT):
                if n + 2 < len(ATT):
                    scores(*ATT[n + 2])
                bk = claim(pe, ("PT", i, h))
                pe.wait_ge(att_exp, n + 1)
                for j in range(i + 1):
                    mm = turn(bk[:, j * P:(j + 1) * P], Pb[n % 3][:, j * P:(j + 1) * P], P)
                made(mm, ("PT", i, h))
                if n >= 1:
                    values(n - 1)
                if n in (1, 3, 5, 7):
                    decode_values(4 + n // 2)
            values(len(ATT) - 1)
            pe.wait_ge(enm_done, 1)
            bk = claim(pe, ("aT",))
            for n, src in enumerate((arow, enm)):
                for i in range(NPT):
                    mm = turn(bk[:, n * 32 + i * H:n * 32 + (i + 1) * H], src[:, i * P:(i + 1) * P], H)
            made(mm, ("aT",))
            for i in range(NPT):
                bk = claim(pe, ("kt", i))
                for c in range(4):
                    mm = turn(bk[:, c * P:(c + 1) * P], qkT[:, 4 + c, i * P:(i + 1) * P], P)
                made(mm, ("kt", i))

            def minus_max(h):
                bk = claim(pe, ("nM", h))
                product(bk[:, :], [(sel[:, h, :], nrow[:, 0:SEQ])], ("nM", h))

            minus_max(0)
            for h in range(H):
                b = h % 2
                if h + 1 < H:
                    minus_max(h + 1)
                ps = slice(64 * b, 64 * b + 64)
                for j in range(NPT):
                    w = (NPT - j) * P
                    bk = claim(pe, ("ST", h, j))
                    product(bk[:, 0:w], [(qkT[ps, 4 + h // 2, j * P:(j + 1) * P], qkT[ps, h // 2, j * P:SEQ])],
                            ("ST", h, j))
                bk = claim(pe, ("num", h))
                for j in range(NPT):
                    emptied(pe, ("ST", h, j))
                if h == 0:
                    for i in range(NPT):
                        emptied(pe, ("mv", i))
                for i in range(NPT):
                    mm = product(bk[:, i * (DH + 1):(i + 1) * (DH + 1)],
                                 [(sdm[b][:, OJ[j] + (i - j) * P:OJ[j] + (i - j + 1) * P], mv1[:, j, h, :])
                                  for j in range(i + 1)])
                made(mm, ("num", h))
                bk = claim(pe, ("C", h))
                pe.wait_ge(ml_wk, NPT * (h + 1))
                product(bk[0:DH + 1, 0:DH], [(mv1[:, j, h, :], wk[b][:, j, :]) for j in range(NPT)], ("C", h))

            for i in range(NPT):
                bk = claim(pe, ("mA", i))
                for c in range(4):
                    mm = turn(bk[:, c * P:(c + 1) * P], atok[:, i, c * P:(c + 1) * P], P)
                made(mm, ("mA", i))
            for i in range(NTT):
                r = rows(i)
                bk = claim(pe, ("mM", i))
                pe.wait_ge(ml_norm, i + 1)
                for c in range(4):
                    mm = turn(bk[:, c * r:(c + 1) * r], hraw[0:r, i, c * P:(c + 1) * P], r)
                made(mm, ("mM", i))
            for i in range(NPT):
                emptied(pe, ("mA", i))
            for i in range(NTT):
                emptied(pe, ("mM", i))
            pe.wait_ge(s_mixed, 1)
            for m in range(KT):
                w = weights_arrived(pe, f"wo{m // 4}")
                for f in range(2):
                    bk = claim(pe, ("wo", m, f))
                    product(bk[:, 0:HALF], [(w[:, k, (m % 4) * P:(m % 4 + 1) * P], mixT[:, k, halves[f]])
                                            for k in range(KT)], ("wo", m, f))
            for f in range(2):
                bk = claim(pe, ("n2", f))
                pe.wait_ge(sq2_done, KT)
                product(bk[:, 0:HALF], [(ones[:, :], sqT[:, k, halves[f]]) for k in range(KT)], ("n2", f))
            pe.wait_ge(h2_done, KT)
            pe.wait_ge(sk_in, 16)

            def query(h):
                for m in (2 * h, 2 * h + 1):
                    w = weights_arrived(pe, f"wq{m // 4}")
                    for f in range(2):
                        bk = claim(pe, ("wq", m, f))
                        product(bk[:, 0:HALF], [(w[:, k, (m % 4) * P:(m % 4 + 1) * P], hT[:, k, halves[f]])
                                                for k in range(KT)], ("wq", m, f))

            for h in range(H):
                for g in queries_before(h):
                    query(g)
                for m in (2 * h, 2 * h + 1):
                    for f in range(2):
                        emptied(pe, ("wq", m, f))
                for i in range(NPT):
                    t = slice(i * P, (i + 1) * P)
                    bk = claim(pe, ("sc", h, i))
                    for a in range(2):
                        product(bk[:, a * P:(a + 1) * P], [(qg[h % 2][:, a, t], skT[:, 2 * h + a, :])])
                    product(bk[:, 256:257], [(qsq[h % 2][:, a, t], ones[:, 0:1]) for a in range(2)], ("sc", h, i))
            bk = claim(pe, ("sc", H, NPT))
            for a in range(2):
                product(bk[0:64, a * P:(a + 1) * P], [(qz[:, a, h, :], skT[:, 2 * h + a, :]) for h in range(H)])
            product(bk[0:64, 256:257], [(qzsq[:, a, h, :], ones[:, 0:1]) for a in range(2) for h in range(H)],
                    ("sc", H, NPT))
            pe.wait_ge(looked, len(UNITS))
            for i in range(NTT):
                bk = claim(pe, ("tb", i))
                pe.wait_ge(tb_done, i + 1)
                if i < NPT:
                    for n, src in enumerate((idx[:, i, 0, :], idx[:, i, 1, :], gt[:, i, :])):
                        mm = turn(bk[:, n * P:(n + 1) * P], src, P)
                    made(mm, ("tb", i))
                else:
                    for n in range(3):
                        mm = product(bk[:, n * DB:(n + 1) * DB], [(byrow[:, n, :], seld)])
                    made(mm, ("tb", i))
            for i in range(NTT):
                emptied(pe, ("tb", i))

            def gates(n, b, i):
                for q in range(QUADS):
                    u = n * QUADS + q
                    if q % 2 == 0:
                        pe.wait_ge(gl_R, n * PAIRS + q // 2 + 1)
                        pe.wait_ge(gl_L, 2 * (n * PAIRS + q // 2 + 1))
                    wait_pos(pe, gl_ev, u - 4)
                    for t in range(4):
                        for part in range(2):
                            mm = pe.matmul(gbank[q % 5][:, t * P:(t + 1) * P], oneR[q // 2][:, q % 2, :, t],
                                           gateL[q // 2][:, part, q % 2, :, t], start=(part == 0), stop=(part == 1))
                    mm.then_inc(gl_mm, 1)

            blocks(pe, gates)

            def up(g):
                b = g.b
                pe.wait_ge(ulo_done, g.n * 4 + 4)
                for c in range(GC):
                    wait_pos(pe, a_gelu, g.n * GC + c - 1)
                    for k in range(KT):
                        for n, (w, hs) in enumerate(((u_hi, h_hi), (u_hi, h_lo), (u_lo, h_hi))):
                            for f in range(2):
                                mm = pe.matmul(abank[c % 2][:, f, 0:HALF], w[b][:, k, c * P:(c + 1) * P],
                                               hs[:, k, halves[f]], start=(k == 0 and n == 0),
                                               stop=(k == KT - 1 and n == 2))
                    mm.then_inc(a_made, 1)

            def down(g):
                b = g.b
                pe.wait_ge(vlo_done, g.n * 4 + 4)
                pe.wait_ge(wlo_done, g.n * GC + GC)
                for m in range(KT):
                    wait_pos(pe, b_added, g.n * KT + m - 1)
                    for c in range(GC):
                        for n, (w, x) in enumerate(((v_hi, w_hi), (v_hi, w_lo), (v_lo, w_hi))):
                            for f in range(2):
                                mm = pe.matmul(bbank[m % 2][:, f, 0:HALF], w[b][:, c, m * P:(m + 1) * P],
                                               x[b][:, c, halves[f]], start=(c == 0 and n == 0),
                                               stop=(c == GC - 1 and n == 2))
                    mm.then_inc(b_made, 1)

            def pe_step(g, last):
                if not (last and g.b == 1):
                    up(g.plus(1))
                down(g)

            pe.wait_ge(gl_ev, NBLK * QUADS)
            up(Group(0, 0))
            groups(pe, pe_step)


def constants():
    import numpy as np

    c = np.zeros((P, C_END), np.float32)
    c[:, C_IDENT:C_IDENT + P] = np.eye(P)
    c[:, C_IOTA:C_IOTA + P] = np.arange(P)
    p = np.arange(P)[:, None]
    dist = 384 + p - np.arange(SEQ)[None, :]
    count = sum(((dist >= 0) & (dist <= w) & (dist % d == 0)).astype(np.int64) for w, d in DIL)
    c[:, C_MASK:C_MASK + SEQ] = np.where(count > 0, np.log(np.maximum(count, 1)), NEG)
    c[:, C_CAUSAL:C_CAUSAL + P] = np.where(np.arange(P)[None, :] >= p, 0.0, NEG)
    inv = (10000.0 ** (-np.arange(32) / 32.0)).astype(np.float32)
    pos = np.full(P * NTT, 4096, np.float32)
    pos[:SEQ] = np.arange(SEQ)
    ang = (pos[:, None] * inv[None, :]).astype(np.float32)
    for at, fn in ((C_COS, np.cos), (C_SIN, np.sin)):
        t = fn(ang.astype(np.float64)).astype(np.float32).reshape(NTT, P, 32)
        c[:, at:at + 160] = t.transpose(1, 0, 2).reshape(P, 160)
    c[0:64, C_SEL:C_SELH] = (np.arange(64)[:, None] // H == np.arange(DB)[None, :])
    c[0:64, C_SELH:C_END] = (np.arange(64)[:, None] % H == np.arange(H)[None, :])
    sel = np.zeros((H, H, P), np.float32)
    for h in range(H):
        sel[h, h, :] = 1.0
    return c, sel


def kernel(x_prompt, x_sample, cache_attn_k, cache_attn_v, state_mlstm_C, state_mlstm_n, state_mlstm_m,
           state_mlstm_conv, norm1_g, w_in, att_qnorm_g, att_knorm_g, b_gates, mlstm_conv_w, mlstm_conv_b,
           mlstm_norm_g, w_out, norm2_g, peer_w_query, peer_qnorm_g, peer_subkeys, peer_u, peer_v):
    import numpy as np
    import concourse.bacc as bacc
    from concourse import mybir as mb
    from concourse.bass_utils import run_bass_kernel_spmd as run

    A = np.ascontiguousarray

    def by_part(w):
        w = np.asarray(w)
        return w.reshape(-1, P, w.shape[-1]).transpose(1, 0, 2)

    x_all = np.concatenate([np.asarray(x_prompt).reshape(SEQ, D), np.asarray(x_sample).reshape(DB, D)])
    w = np.asarray(w_in)[0]
    at = dict(q=0, k=WID, v=2 * WID, mqk0=3 * WID, mqk1=4 * WID, mv=5 * WID, mo=6 * WID + 16)
    wo, wq = np.asarray(w_out)[0], np.asarray(peer_w_query)[0]
    groups = []
    for g in WGROUPS:
        if g in at:
            groups.append(w[:, at[g]:at[g] + 512])
        else:
            src = wo if g[:2] == "wo" else wq
            n = int(g[2:])
            groups.append(src[:, n * 512:(n + 1) * 512])
    const, sel = constants()
    par = np.zeros((P, P_END), np.float32)
    par[:, P_G1:P_G1 + 8] = np.asarray(norm1_g)[0].reshape(KT, P).T
    par[:, P_G2:P_G2 + 8] = np.asarray(norm2_g)[0].reshape(KT, P).T
    par[:, P_GQN:P_GQN + 2] = np.asarray(peer_qnorm_g)[0].reshape(2, P).T
    par[:, P_CW:P_CW + 32] = np.asarray(mlstm_conv_w)[0].reshape(CW, KT, P).transpose(2, 1, 0).reshape(P, 32)
    par[:, P_CB:P_CB + 8] = np.asarray(mlstm_conv_b)[0].reshape(KT, P).T
    par[:, P_GQ:P_GQ + DH] = np.asarray(att_qnorm_g)[0]
    par[:, P_GK:P_GK + DH] = np.asarray(att_knorm_g)[0]
    par[:, P_GM:P_GM + WID] = np.asarray(mlstm_norm_g)[0]
    par[0:H, P_BG8:P_BG8 + 2] = np.asarray(b_gates)[0].reshape(2, H).T
    par[:, P_M0] = np.repeat(np.asarray(state_mlstm_m)[0].reshape(-1), 2)
    par[:, P_N0:P_N0 + DH] = np.repeat(np.asarray(state_mlstm_n)[0].reshape(-1, DH), 2, axis=0)
    ins = dict(
        const=const, par=par, sel=sel,
        xT=A(by_part(x_all.T)),
        wg=A(by_part(w[:, 6 * WID:6 * WID + 16])),
        w=A(np.stack([by_part(g) for g in groups])),
        cst=A(np.asarray(state_mlstm_conv)[0].reshape(DB, 3, KT, P).transpose(3, 2, 1, 0)),
        ck=A(np.asarray(cache_attn_k)[0].reshape(DB, NCACHE, WID)),
        cv=A(np.asarray(cache_attn_v)[0].reshape(DB, NCACHE, WID)),
        C0=A(np.asarray(state_mlstm_C)[0].reshape(P, 32, DH)),
        sk=A(np.asarray(peer_subkeys)[0].reshape(2 * H, NKEYS, P).transpose(2, 0, 1)),
        uT=A(np.asarray(peer_u)[0].reshape(NG, GC * P, KT, P).transpose(0, 3, 2, 1).reshape(NG, P, KT * GC * P)),
        v=A(np.asarray(peer_v)[0].reshape(NG, GC, P, D).transpose(0, 2, 1, 3).reshape(NG, P, GC * D)),
    )
    outs = dict(
        yT=(P, KT, NT), kp=(NPT, P, WID), vp=(NPT, P, WID), ks=(DB, WID), vs=(DB, WID),
        Cp=(H, DH, DH), np=(1, H, DH), mp=(H, 1), convp=(P, KT, 3), convs=(P, KT, 3, DB),
        Cs=(P, 32, DH), ns=(DB * H, DH), ms=(DB * H, 1),
    )
    nc = bacc.Bacc("TRN2", target_bir_lowering=False, num_devices=1)
    arrays = {f"in_{n}": a for n, a in ins.items()}
    I = {n: nc.dram_tensor(f"in_{n}", a.shape, mb.dt.from_np(a.dtype), kind="ExternalInput").ap() for n, a in ins.items()}
    O = {n: nc.dram_tensor(f"out_{n}", s, F32, kind="ExternalOutput").ap() for n, s in outs.items()}
    trunk_and_peer(nc, I, O)
    r = run(nc, [arrays], core_ids=[0]).results[0]
    o = {n: r[f"out_{n}"] for n in outs}
    y = o["yT"].transpose(2, 1, 0).reshape(NT, D)
    return (
        A(y[:SEQ]).reshape(1, SEQ, D), A(y[SEQ:]).reshape(DB, 1, D),
        o["kp"].reshape(1, 1, SEQ, H, DH), o["vp"].reshape(1, 1, SEQ, H, DH),
        o["ks"].reshape(1, DB, 1, H, DH), o["vs"].reshape(1, DB, 1, H, DH),
        o["Cp"].reshape(1, 1, H, DH, DH), o["np"].reshape(1, 1, H, DH), o["mp"].reshape(1, 1, H),
        A(o["convp"].transpose(2, 1, 0)).reshape(1, 1, 3, D),
        o["Cs"].reshape(1, DB, H, DH, DH), o["ns"].reshape(1, DB, H, DH), o["ms"].reshape(1, DB, H),
        A(o["convs"].transpose(3, 2, 1, 0)).reshape(1, DB, 3, D),
    )
```
